# Optimizing a Trainium2 kernel written in Bass

```python
import math
import jax, jax.numpy as jnp
from jax import lax
import numpy as np

D_MODEL = 1024
BATCH = 1
SEQ = 256
DEPTH = 2

CHUNK = 64
EPS = 1e-6

GM_WIDTH = 1024
GM_GROUPS = 4
GM_BLOCK = 128

MLA_HEADS = 8
MLA_NOPE = 128
MLA_ROPE = 64
MLA_VDIM = 128
MLA_QK_DIM = MLA_NOPE + MLA_ROPE
MLA_Q_RANK = 384
MLA_KV_RANK = 256
MLA_WIDTH = MLA_HEADS * MLA_VDIM
ROPE_THETA = 10000.0
Q_BLOCK = 128

LRU_WIDTH = 1280
LRU_BLOCKS = 16
LRU_BW = LRU_WIDTH // LRU_BLOCKS
LRU_C = 8.0
CONV_W = 4

IN_SIZES = (GM_WIDTH, GM_WIDTH, GM_WIDTH, MLA_Q_RANK, MLA_KV_RANK, MLA_ROPE, MLA_WIDTH,
            LRU_WIDTH, LRU_WIDTH, D_MODEL, D_MODEL, D_MODEL)
N_IN = sum(IN_SIZES)


def _split_points():
    return [int(s) for s in np.cumsum(IN_SIZES)[:-1]]

def rmsnorm(x, g):
    xf = x.astype(jnp.float32)
    y = xf * lax.rsqrt(jnp.mean(xf * xf, axis=-1, keepdims=True) + EPS)
    return (y * g.astype(jnp.float32)).astype(x.dtype)

def layernorm(x, g, b):
    xf = x.astype(jnp.float32)
    mu = jnp.mean(xf, axis=-1, keepdims=True)
    var = jnp.mean(jnp.square(xf - mu), axis=-1, keepdims=True)
    y = (xf - mu) * lax.rsqrt(var + EPS)
    return (y * g.astype(jnp.float32) + b.astype(jnp.float32)).astype(x.dtype)

def rope(t, cos, sin):
    half = t.shape[-1] // 2
    t1, t2 = t[..., :half], t[..., half:]
    return jnp.concatenate([t1 * cos - t2 * sin, t2 * cos + t1 * sin], axis=-1)

def gmlp_spatial(u, v, ln_g, ln_b, ws, bs):
    B, S, _ = v.shape
    v = layernorm(v, ln_g, ln_b)
    vb = v.reshape(B, S // GM_BLOCK, GM_BLOCK, GM_GROUPS, GM_WIDTH // GM_GROUPS)
    idx = jnp.arange(GM_BLOCK)
    mask = (idx[None, :] // CHUNK) <= (idx[:, None] // CHUNK)
    ws_m = jnp.where(mask[None], ws, jnp.zeros_like(ws))
    sv = jnp.einsum('gij,bnjgc->bnigc', ws_m, vb) + bs.T[None, None, :, :, None]
    return u * sv.reshape(B, S, GM_WIDTH)

def mla_attention(c_q, c_kv, k_rope_in, q_norm_g, w_uq, kv_norm_g, w_ukv):
    B, S, _ = c_q.shape
    H = MLA_HEADS
    q = (rmsnorm(c_q, q_norm_g) @ w_uq).reshape(B, S, H, MLA_QK_DIM)
    kv = (rmsnorm(c_kv, kv_norm_g) @ w_ukv).reshape(B, S, H, MLA_NOPE + MLA_VDIM)
    q_nope, q_rope = q[..., :MLA_NOPE], q[..., MLA_NOPE:]
    k_nope, v = kv[..., :MLA_NOPE], kv[..., MLA_NOPE:]

    pos = jnp.arange(S, dtype=jnp.float32)
    inv_freq = ROPE_THETA ** (-jnp.arange(0, MLA_ROPE, 2, dtype=jnp.float32) / MLA_ROPE)
    ang = pos[:, None] * inv_freq[None, :]
    cos = jnp.cos(ang).astype(q.dtype)
    sin = jnp.sin(ang).astype(q.dtype)
    q_rope = rope(q_rope, cos[None, :, None, :], sin[None, :, None, :])
    k_rope = rope(k_rope_in, cos[None], sin[None])

    q = jnp.concatenate([q_nope, q_rope], axis=-1)
    k = jnp.concatenate([k_nope, jnp.broadcast_to(k_rope[:, :, None, :], (B, S, H, MLA_ROPE))], axis=-1)
    scale = 1.0 / math.sqrt(MLA_QK_DIM)
    nb = S // Q_BLOCK
    qb = q.reshape(B, nb, Q_BLOCK, H, MLA_QK_DIM).transpose(1, 0, 2, 3, 4)
    key_chunk = jnp.arange(S) // CHUNK

    def one_block(args):
        qi, bi = args
        s = jnp.einsum('bqhd,bkhd->bhqk', qi, k).astype(jnp.float32) * scale
        q_chunk = (bi * Q_BLOCK + jnp.arange(Q_BLOCK)) // CHUNK
        mask = key_chunk[None, :] <= q_chunk[:, None]
        s = jnp.where(mask[None, None], s, -1e30)
        p = jax.nn.softmax(s, axis=-1).astype(v.dtype)
        return jnp.einsum('bhqk,bkhd->bqhd', p, v)

    o = lax.map(one_block, (qb, jnp.arange(nb)))
    return o.transpose(1, 0, 2, 3, 4).reshape(B, S, MLA_WIDTH)

def rg_lru(x_c, conv_w, conv_b, w_a, b_a, w_x, b_x, lam):
    B, S, C = x_c.shape
    xc = lax.conv_general_dilated(
        x_c, conv_w[:, None, :].astype(x_c.dtype), window_strides=(1,), padding=[(CONV_W - 1, 0)],
        dimension_numbers=('NWC', 'WIO', 'NWC'), feature_group_count=C) + conv_b
    xb = xc.reshape(B, S, LRU_BLOCKS, LRU_BW)
    r = jax.nn.sigmoid(jnp.einsum('bshi,hij->bshj', xb, w_a).reshape(B, S, C) + b_a)
    i = jax.nn.sigmoid(jnp.einsum('bshi,hij->bshj', xb, w_x).reshape(B, S, C) + b_x)
    rf = r.astype(jnp.float32)
    log_a = -LRU_C * rf * jax.nn.softplus(-lam.astype(jnp.float32))
    a = jnp.exp(log_a)
    mult = jnp.sqrt(jnp.maximum(1.0 - jnp.exp(2.0 * log_a), 0.0))
    bterm = mult * (i.astype(jnp.float32) * xc.astype(jnp.float32))

    def combine(e1, e2):
        a1, b1 = e1
        a2, b2 = e2
        return a1 * a2, a2 * b1 + b2

    _, h = lax.associative_scan(combine, (a, bterm), axis=1)
    return h.astype(x_c.dtype)

def first_inputs(seed: int = 0) -> dict:
    key = jax.random.key(seed)
    ks = iter(jax.random.split(key, 32))
    L, D = DEPTH, D_MODEL

    def nrm(shape, scale):
        return jax.random.normal(next(ks), shape, jnp.float32) * scale

    def gain(shape):
        return 1.0 + nrm(shape, 0.02)

    a_init = jax.random.uniform(next(ks), (L, LRU_WIDTH), jnp.float32, 0.9, 0.999)
    s = a_init ** (1.0 / LRU_C)
    lam = jnp.log(s) - jnp.log1p(-s)

    return {
        "x": nrm((BATCH, SEQ, D), 1.0),
        "pre_norm_g": gain((L, D)),
        "w_in": nrm((L, D, N_IN), D ** -0.5),
        "gm_ln_g": gain((L, GM_WIDTH)),
        "gm_ln_b": nrm((L, GM_WIDTH), 0.02),
        "gm_ws": nrm((L, GM_GROUPS, GM_BLOCK, GM_BLOCK), GM_BLOCK ** -0.5),
        "gm_bs": 1.0 + nrm((L, GM_GROUPS, GM_BLOCK), 0.02),
        "mla_q_norm_g": gain((L, MLA_Q_RANK)),
        "mla_w_uq": nrm((L, MLA_Q_RANK, MLA_HEADS * MLA_QK_DIM), MLA_Q_RANK ** -0.5),
        "mla_kv_norm_g": gain((L, MLA_KV_RANK)),
        "mla_w_ukv": nrm((L, MLA_KV_RANK, MLA_HEADS * (MLA_NOPE + MLA_VDIM)), MLA_KV_RANK ** -0.5),
        "lru_conv_w": nrm((L, CONV_W, LRU_WIDTH), CONV_W ** -0.5),
        "lru_conv_b": nrm((L, LRU_WIDTH), 0.01),
        "lru_w_a": nrm((L, LRU_BLOCKS, LRU_BW, LRU_BW), LRU_BW ** -0.5),
        "lru_b_a": nrm((L, LRU_WIDTH), 0.01),
        "lru_w_x": nrm((L, LRU_BLOCKS, LRU_BW, LRU_BW), LRU_BW ** -0.5),
        "lru_b_x": nrm((L, LRU_WIDTH), 0.01),
        "lru_lambda": lam,
        "w_proj_a": nrm((L, GM_WIDTH, D), GM_WIDTH ** -0.5),
        "w_proj_b": nrm((L, MLA_WIDTH, D), MLA_WIDTH ** -0.5),
        "w_proj_c": nrm((L, LRU_WIDTH, D), LRU_WIDTH ** -0.5),
        "w_out": nrm((L, D, D), D ** -0.5),
        "post_norm_g": gain((L, D)),
    }

def first_block(x, pre_norm_g, w_in, gm_ln_g, gm_ln_b, gm_ws, gm_bs, mla_q_norm_g, mla_w_uq,
              mla_kv_norm_g, mla_w_ukv, lru_conv_w, lru_conv_b, lru_w_a, lru_b_a, lru_w_x,
              lru_b_x, lru_lambda, w_proj_a, w_proj_b, w_proj_c, w_out, post_norm_g):
    cuts = _split_points()
    for l in range(DEPTH):
        h = rmsnorm(x, pre_norm_g[l])
        proj = h @ w_in[l]
        (u, v, z_a, c_q, c_kv, k_rope, z_b, x_c, z_c,
         g_a, g_b, g_c) = jnp.split(proj, cuts, axis=-1)

        y_a = gmlp_spatial(u, v, gm_ln_g[l], gm_ln_b[l], gm_ws[l], gm_bs[l]) * jax.nn.silu(z_a)
        y_b = mla_attention(c_q, c_kv, k_rope, mla_q_norm_g[l], mla_w_uq[l],
                            mla_kv_norm_g[l], mla_w_ukv[l]) * jax.nn.silu(z_b)
        y_c = rg_lru(x_c, lru_conv_w[l], lru_conv_b[l], lru_w_a[l], lru_b_a[l],
                     lru_w_x[l], lru_b_x[l], lru_lambda[l]) * jax.nn.silu(z_c)

        merged = (jax.nn.sigmoid(g_a) * (y_a @ w_proj_a[l])
                  + jax.nn.sigmoid(g_b) * (y_b @ w_proj_b[l])
                  + jax.nn.sigmoid(g_c) * (y_c @ w_proj_c[l]))
        x = x + rmsnorm(merged @ w_out[l], post_norm_g[l])
    return x


N_A = DEPTH // 2
N_B = DEPTH - N_A
POOL_WINDOWS = (2, 4, 8, 16)
POOL_GROUP = D_MODEL // len(POOL_WINDOWS)
N_HEADS = 16
HEAD_DIM = 64
N_KV_GROUPS = 4
HEADS_PER_GROUP = N_HEADS // N_KV_GROUPS
CMP_STRIDE = 16
CMP_LEN = 2 * CMP_STRIDE
CMP_HIDDEN = 128
SLC_BLOCK = 64
N_SELECT = 16
WINDOW = 512
Q_BLOCK_2 = 64
N_BRANCH = 3
ROPE_THETA_2 = 500000.0
ROT_DIM = HEAD_DIM // 4
D_FF = 2816
CONV_W_2 = 3
PLE_DIM = 256

NEG = -1e30
FORCE_SCORE = 1e4


def rmsnorm_2(x, g):
    xf = x.astype(jnp.float32)
    y = xf * lax.rsqrt(jnp.mean(xf * xf, axis=-1, keepdims=True) + EPS) * g.astype(jnp.float32)
    return y.astype(x.dtype)

def rope_tables(pos):
    inv_freq = ROPE_THETA_2 ** (-jnp.arange(0, ROT_DIM, 2, dtype=jnp.float32) / ROT_DIM)
    ang = pos.astype(jnp.float32)[..., None] * inv_freq
    return jnp.cos(ang), jnp.sin(ang)

def rope_2(x, cos, sin):
    xf = x.astype(jnp.float32)
    half = ROT_DIM // 2
    x1, x2, xp = xf[..., :half], xf[..., half:ROT_DIM], xf[..., ROT_DIM:]
    out = jnp.concatenate([x1 * cos - x2 * sin, x2 * cos + x1 * sin, xp], axis=-1)
    return out.astype(x.dtype)

def masked_softmax(s, mask):
    s = jnp.where(mask, s, NEG)
    m = jnp.max(s, axis=-1, keepdims=True)
    e = jnp.where(mask, jnp.exp(s - m), 0.0)
    return e / jnp.maximum(jnp.sum(e, axis=-1, keepdims=True), 1e-30)

def pool_mixer(h, w, scale):
    B, S, D = h.shape
    c = jnp.cumsum(h.astype(jnp.float32), axis=1)
    c = jnp.pad(c, ((0, 0), (1, 0), (0, 0)))
    t = jnp.arange(S)
    outs = []
    for gi, win in enumerate(POOL_WINDOWS):
        sl = slice(gi * POOL_GROUP, (gi + 1) * POOL_GROUP)
        cg = c[..., sl]
        lo = jnp.maximum(t + 1 - win, 0)
        cnt = jnp.minimum(t + 1, win).astype(jnp.float32)
        avg = (cg[:, t + 1] - cg[:, lo]) / cnt[:, None]
        u = (avg - h[..., sl].astype(jnp.float32)).astype(h.dtype)
        outs.append(jnp.einsum('bsc,cd->bsd', u, w[gi]))
    return jnp.concatenate(outs, axis=-1) * scale

def conv_ffn(h, w_up, conv_w, conv_b, w_down):
    S = h.shape[1]
    u = h @ w_up
    up = jnp.pad(u, ((0, 0), (CONV_W_2 - 1, 0), (0, 0)))
    u = sum(conv_w[j] * up[:, j:j + S] for j in range(CONV_W_2)) + conv_b
    a, g = u[..., :D_FF], u[..., D_FF:]
    return (jax.nn.silu(g) * a) @ w_down

def compress(blocks, pos_emb, w1, w2):
    z = blocks + pos_emb
    z = z.reshape(z.shape[:3] + (CMP_LEN * HEAD_DIM,))
    return jax.nn.gelu(z @ w1) @ w2

def nsa_shared_kv(x, positions, norm_kv, w_kv, cmp_pos_k, cmp_w1_k, cmp_w2_k, cmp_pos_v, cmp_w1_v, cmp_w2_v):
    B, S, _ = x.shape
    h = rmsnorm_2(x, norm_kv)
    kv = (h @ w_kv).reshape(B, S, 2 * N_BRANCH, N_KV_GROUPS, HEAD_DIM).transpose(2, 0, 3, 1, 4)
    k_c, v_c, k_s, v_s, k_w, v_w = [kv[i] for i in range(2 * N_BRANCH)]
    cos, sin = rope_tables(positions)
    k_s = rope_2(k_s, cos[:, None], sin[:, None])
    k_w = rope_2(k_w, cos[:, None], sin[:, None])
    n_chunk = S // CMP_STRIDE
    n_cmp = n_chunk - 1
    def blocks_of(z):
        ch = z.reshape(B, N_KV_GROUPS, n_chunk, CMP_STRIDE, HEAD_DIM)
        return jnp.concatenate([ch[:, :, :-1], ch[:, :, 1:]], axis=3)
    kc = compress(blocks_of(k_c), cmp_pos_k, cmp_w1_k, cmp_w2_k)
    vc = compress(blocks_of(v_c), cmp_pos_v, cmp_w1_v, cmp_w2_v)
    end_idx = CMP_STRIDE * jnp.arange(n_cmp) + CMP_LEN - 1
    cos_c, sin_c = rope_tables(positions[:, end_idx])
    kc = rope_2(kc, cos_c[:, None], sin_c[:, None])
    n_slc = S // SLC_BLOCK
    ks_blk = k_s.reshape(B, N_KV_GROUPS, n_slc, SLC_BLOCK, HEAD_DIM)
    vs_blk = v_s.reshape(B, N_KV_GROUPS, n_slc, SLC_BLOCK, HEAD_DIM)
    pad = ((0, 0), (0, 0), (WINDOW, 0), (0, 0))
    kw_pad, vw_pad = jnp.pad(k_w, pad), jnp.pad(v_w, pad)
    return (kc, vc, ks_blk, vs_blk, kw_pad, vw_pad)

def nsa_attention(h, w_in, w_out, cos, sin, kv):
    kc, vc, ks_blk, vs_blk, kw_pad, vw_pad = kv
    B, S, _ = h.shape
    n_cmp = kc.shape[2]
    n_slc = ks_blk.shape[2]
    n_top = min(N_SELECT, n_slc)
    scale = HEAD_DIM ** -0.5
    proj = h @ w_in
    q = proj[..., :N_HEADS * HEAD_DIM].reshape(B, S, N_HEADS, HEAD_DIM)
    q = rope_2(q, cos[:, :, None], sin[:, :, None])
    q = q.reshape(B, S, N_KV_GROUPS, HEADS_PER_GROUP, HEAD_DIM).transpose(0, 2, 3, 1, 4)
    gates = jax.nn.sigmoid(proj[..., N_HEADS * HEAD_DIM:].astype(jnp.float32))
    gates = gates.reshape(B, S, N_KV_GROUPS, HEADS_PER_GROUP, N_BRANCH).transpose(0, 2, 3, 1, 4)

    c_idx = jnp.arange(n_cmp)
    c_end = CMP_STRIDE * c_idx + CMP_LEN - 1
    blk = jnp.arange(n_slc)
    c_start = CMP_STRIDE * c_idx
    overlap = ((c_start[:, None] < (blk[None] + 1) * SLC_BLOCK)
               & (c_start[:, None] + CMP_LEN > blk[None] * SLC_BLOCK)).astype(jnp.float32)
    gather = jax.vmap(jax.vmap(lambda kb, ix: kb[ix]))

    def block_fn(s):
        t = s + jnp.arange(Q_BLOCK_2)
        qb = lax.dynamic_slice_in_dim(q, s, Q_BLOCK_2, axis=3)
        gb = lax.dynamic_slice_in_dim(gates, s, Q_BLOCK_2, axis=3)
        sc = jnp.einsum('bghqd,bgcd->bghqc', qb, kc).astype(jnp.float32) * scale
        p_c = masked_softmax(sc, c_end[None, :] <= t[:, None])
        o_c = jnp.einsum('bghqc,bgcd->bghqd', p_c.astype(vc.dtype), vc)
        imp = jnp.einsum('bghqc,cn->bgqn', p_c, overlap)
        cur = t // SLC_BLOCK
        forced = (blk[None] == 0) | (blk[None] == cur[:, None]) | (blk[None] == cur[:, None] - 1)
        valid = blk[None] * SLC_BLOCK <= t[:, None]
        score = jnp.where(valid, jnp.where(forced, FORCE_SCORE, imp), NEG)
        vals, idx = lax.top_k(score, n_top)
        ok = vals > 0.5 * NEG
        ks_g = gather(ks_blk, idx).reshape(B, N_KV_GROUPS, Q_BLOCK_2, n_top * SLC_BLOCK, HEAD_DIM)
        vs_g = gather(vs_blk, idx).reshape(B, N_KV_GROUPS, Q_BLOCK_2, n_top * SLC_BLOCK, HEAD_DIM)
        kpos = idx[..., None] * SLC_BLOCK + jnp.arange(SLC_BLOCK)
        mask_s = (ok[..., None] & (kpos <= t[:, None, None])).reshape(B, N_KV_GROUPS, Q_BLOCK_2, n_top * SLC_BLOCK)
        ss = jnp.einsum('bghqd,bgqkd->bghqk', qb, ks_g).astype(jnp.float32) * scale
        p_s = masked_softmax(ss, mask_s[:, :, None])
        o_s = jnp.einsum('bghqk,bgqkd->bghqd', p_s.astype(vs_g.dtype), vs_g)
        kw = lax.dynamic_slice_in_dim(kw_pad, s, WINDOW + Q_BLOCK_2, axis=2)
        vw = lax.dynamic_slice_in_dim(vw_pad, s, WINDOW + Q_BLOCK_2, axis=2)
        kpos_w = s - WINDOW + jnp.arange(WINDOW + Q_BLOCK_2)
        diff = t[:, None] - kpos_w[None]
        mask_w = (diff >= 0) & (diff < WINDOW) & (kpos_w[None] >= 0)
        sw = jnp.einsum('bghqd,bgkd->bghqk', qb, kw).astype(jnp.float32) * scale
        p_w = masked_softmax(sw, mask_w)
        o_w = jnp.einsum('bghqk,bgkd->bghqd', p_w.astype(vw.dtype), vw)
        out = (gb[..., 0:1] * o_c.astype(jnp.float32) + gb[..., 1:2] * o_s.astype(jnp.float32)
               + gb[..., 2:3] * o_w.astype(jnp.float32))
        return out.astype(h.dtype)

    starts = jnp.arange(S // Q_BLOCK_2) * Q_BLOCK_2
    o = lax.map(block_fn, starts)
    o = o.transpose(1, 0, 4, 2, 3, 5).reshape(B, S, N_HEADS * HEAD_DIM)
    return o @ w_out

def second_inputs(seed: int = 0) -> dict:
    key = jax.random.key(seed)
    ks = iter(jax.random.split(key, 40))
    f32 = jnp.float32
    def w(shape, fan):
        return jax.random.normal(next(ks), shape, f32) * (fan ** -0.5)
    def gain(shape):
        return 1.0 + 0.05 * jax.random.normal(next(ks), shape, f32)
    def small(shape, s=0.02):
        return s * jax.random.normal(next(ks), shape, f32)
    q_cols = N_HEADS * HEAD_DIM + N_HEADS * N_BRANCH
    return {
        "x": jax.random.normal(next(ks), (BATCH, SEQ, D_MODEL), f32),
        "p": jax.random.normal(next(ks), (DEPTH, BATCH, SEQ, PLE_DIM), f32),
        "positions": jnp.broadcast_to(jnp.arange(SEQ, dtype=jnp.int32), (BATCH, SEQ)),
        "norm_mix": gain((DEPTH, D_MODEL)),
        "pool_w": w((N_A, len(POOL_WINDOWS), POOL_GROUP, POOL_GROUP), POOL_GROUP),
        "pool_scale": gain((N_A, D_MODEL)),
        "norm_kv": gain((D_MODEL,)),
        "w_kv": w((D_MODEL, 2 * N_BRANCH * N_KV_GROUPS * HEAD_DIM), D_MODEL),
        "cmp_pos_k": small((CMP_LEN, HEAD_DIM), 0.1),
        "cmp_w1_k": w((CMP_LEN * HEAD_DIM, CMP_HIDDEN), CMP_LEN * HEAD_DIM),
        "cmp_w2_k": w((CMP_HIDDEN, HEAD_DIM), CMP_HIDDEN),
        "cmp_pos_v": small((CMP_LEN, HEAD_DIM), 0.1),
        "cmp_w1_v": w((CMP_LEN * HEAD_DIM, CMP_HIDDEN), CMP_LEN * HEAD_DIM),
        "cmp_w2_v": w((CMP_HIDDEN, HEAD_DIM), CMP_HIDDEN),
        "w_in_b": w((N_B, D_MODEL, q_cols), D_MODEL),
        "w_out_b": w((N_B, N_HEADS * HEAD_DIM, D_MODEL), N_HEADS * HEAD_DIM),
        "norm_ffn": gain((DEPTH, D_MODEL)),
        "ffn_up": w((DEPTH, D_MODEL, 2 * D_FF), D_MODEL),
        "ffn_conv": w((DEPTH, CONV_W_2, 2 * D_FF), CONV_W_2),
        "ffn_conv_b": small((DEPTH, 2 * D_FF)),
        "ffn_down": w((DEPTH, D_FF, D_MODEL), D_FF),
        "norm_ple": gain((DEPTH, D_MODEL)),
        "ple_gate": w((DEPTH, D_MODEL, D_MODEL), D_MODEL),
        "ple_proj": w((DEPTH, PLE_DIM, D_MODEL), PLE_DIM),
        "norm_final": gain((D_MODEL,)),
    }

def second_block(x, p, positions, norm_mix, pool_w, pool_scale, norm_kv, w_kv,
              cmp_pos_k, cmp_w1_k, cmp_w2_k, cmp_pos_v, cmp_w1_v, cmp_w2_v,
              w_in_b, w_out_b, norm_ffn, ffn_up, ffn_conv, ffn_conv_b, ffn_down,
              norm_ple, ple_gate, ple_proj, norm_final):
    cos, sin = rope_tables(positions)
    kv = None
    for i in range(DEPTH):
        if i < N_A:
            x = x + pool_mixer(rmsnorm_2(x, norm_mix[i]), pool_w[i], pool_scale[i])
        else:
            if i == N_A:
                kv = nsa_shared_kv(x, positions, norm_kv, w_kv, cmp_pos_k, cmp_w1_k, cmp_w2_k,
                                   cmp_pos_v, cmp_w1_v, cmp_w2_v)
            j = i - N_A
            x = x + nsa_attention(rmsnorm_2(x, norm_mix[i]), w_in_b[j], w_out_b[j], cos, sin, kv)
        x = x + conv_ffn(rmsnorm_2(x, norm_ffn[i]), ffn_up[i], ffn_conv[i], ffn_conv_b[i], ffn_down[i])
        gate = jax.nn.sigmoid(rmsnorm_2(x, norm_ple[i]) @ ple_gate[i])
        x = x + gate * (p[i] @ ple_proj[i])
    return rmsnorm_2(x, norm_final)


def setup_inputs(seed=0):
    out = dict(first_inputs(seed))
    for name, value in second_inputs(seed + 1).items():
        if name != "x":
            out[name + "_2"] = value
    return out


def reference(
    x, pre_norm_g, w_in, gm_ln_g, gm_ln_b, gm_ws, gm_bs, mla_q_norm_g, mla_w_uq, mla_kv_norm_g,
    mla_w_ukv, lru_conv_w, lru_conv_b, lru_w_a, lru_b_a, lru_w_x, lru_b_x, lru_lambda, w_proj_a,
    w_proj_b, w_proj_c, w_out, post_norm_g, p_2, positions_2, norm_mix_2, pool_w_2,
    pool_scale_2, norm_kv_2, w_kv_2, cmp_pos_k_2, cmp_w1_k_2, cmp_w2_k_2, cmp_pos_v_2,
    cmp_w1_v_2, cmp_w2_v_2, w_in_b_2, w_out_b_2, norm_ffn_2, ffn_up_2, ffn_conv_2, ffn_conv_b_2,
    ffn_down_2, norm_ple_2, ple_gate_2, ple_proj_2, norm_final_2,
):
    x = first_block(
        x, pre_norm_g, w_in, gm_ln_g, gm_ln_b, gm_ws, gm_bs, mla_q_norm_g, mla_w_uq,
        mla_kv_norm_g, mla_w_ukv, lru_conv_w, lru_conv_b, lru_w_a, lru_b_a, lru_w_x, lru_b_x,
        lru_lambda, w_proj_a, w_proj_b, w_proj_c, w_out, post_norm_g,
    )
    return second_block(
        x, p_2, positions_2, norm_mix_2, pool_w_2, pool_scale_2, norm_kv_2, w_kv_2, cmp_pos_k_2,
        cmp_w1_k_2, cmp_w2_k_2, cmp_pos_v_2, cmp_w1_v_2, cmp_w2_v_2, w_in_b_2, w_out_b_2,
        norm_ffn_2, ffn_up_2, ffn_conv_2, ffn_conv_b_2, ffn_down_2, norm_ple_2, ple_gate_2,
        ple_proj_2, norm_final_2,
    )


_drawn_inputs = setup_inputs


def setup_inputs(seed=0):
    import zlib

    import numpy as np

    out = dict(_drawn_inputs(seed))
    spreads = {}
    factors = {'gm_ln_g': 4.464,
     'gm_ln_b': 4.127,
     'gm_bs': 3.979,
     'mla_q_norm_g': 8.0,
     'mla_kv_norm_g': 8.0,
     'lru_b_a': 42.332,
     'lru_b_x': 24.612,
     'norm_kv_2': 8.0,
     'cmp_pos_k_2': 8.0,
     'cmp_pos_v_2': 4.129,
     'ffn_conv_b_2': 4.882,
     'norm_ple_2': 8.0}
    for name, (base, spread) in spreads.items():
        noise = np.random.default_rng([zlib.crc32(name.encode()), seed]).standard_normal(out[name].shape)
        drawn = base * np.exp(spread * noise) if base else spread * noise
        out[name] = __import__('jax').numpy.asarray(drawn.astype(out[name].dtype))
    for name, factor in factors.items():
        out[name] = (out[name] * factor).astype(out[name].dtype)
    return out
```

```python
import math
from collections import defaultdict
from contextlib import ExitStack, contextmanager

import numpy as np
import concourse.bass as bass
from concourse import mybir

F32 = mybir.dt.float32
F32R = mybir.dt.float32r
I32 = mybir.dt.int32
ACT = mybir.ActivationFunctionType
ALU = mybir.AluOpType
AX = mybir.AxisListType

P = 128
D = 1024
TOK = 256
TT = TOK // P
KT = D // P
L = 2
EPS = 1e-6
GM = 1024
GM_GROUPS = 4
QR, KVR, ROPE, NOPE, VD, HEADS = 384, 256, 64, 128, 128, 8
QKD = NOPE + ROPE
LRU = 1280
LT = LRU // P
BW = 80
REP = 640
CONV1 = 4
COL_U, COL_V, COL_ZA = 0, GM, 2 * GM
COL_CQ = 3 * GM
COL_CKV = COL_CQ + QR
COL_KR = COL_CKV + KVR
COL_ZB = COL_KR + ROPE
COL_XC = COL_ZB + HEADS * VD
COL_ZC = COL_XC + LRU
COL_GA = COL_ZC + LRU
COL_GB = COL_GA + D
COL_GC = COL_GB + D
SLOT = 2048
HALF = SLOT // 2
SW = 256

FF = 2816
FT = FF // P
PLE = 256
NH, HD, NG = 16, 64, 4
NCMP = 15
SCALE2 = HD ** -0.5

ROW2 = {}
_at = 2 * P
for _name, _n in (("mix", L * KT), ("scale", KT), ("kv", KT), ("ffn", L * KT), ("ple", L * KT), ("final", KT),
                  ("posk", 16), ("posv", 16)):
    ROW2[_name] = _at
    _at += _n


def conv_row(l, tap):
    return (3 + 2 * l + tap // 2) * P + (tap % 2) * 2 * FT
ROW_LOADS = 32

PAIRS = [(o, i) for o in range(REP // P) for i in range(REP // P)
         if any(b * BW < (o + 1) * P and (b + 1) * BW > o * P and b * BW < (i + 1) * P and (b + 1) * BW > i * P
                for b in range(REP // BW))]


def gate_pieces():
    out = []
    for b in range(REP // BW):
        cuts = [b * BW] + [c for c in range(P, REP, P) if b * BW < c < (b + 1) * BW] + [(b + 1) * BW]
        for r0, r1 in zip(cuts, cuts[1:]):
            for c0, c1 in zip(cuts, cuts[1:]):
                out.append((PAIRS.index((c0 // P, r0 // P)), r0 % P, r0 - b * BW, r1 - r0,
                            c0 % P, c0 - b * BW, c1 - c0, b))
    return out


CONST = {}
_at = 0
for _name, _n in (("ident", P), ("ones", P), ("swap1", P), ("swap2", P), ("cos1", TOK), ("sin1", TOK),
                  ("mask1", TOK), ("mask0", P), ("causal1", TOK), ("cmp1", 16), ("cmp0", 16), ("cmo1", 16), ("cmo0", 16),
                  ("count", 64), ("freq", 4)):
    CONST[_name] = (_at, _at + _n)
    _at += _n
NCONST = _at


def shape_constants():
    c = np.zeros((P, NCONST), np.float32)

    def put(name, value):
        c[:, CONST[name][0]:CONST[name][1]] = value
    put("ident", np.eye(P))
    put("ones", 1.0)
    s = np.zeros((P, P))
    for h in (0, 64):
        for i in range(32):
            s[h + i, h + 32 + i] = s[h + 32 + i, h + i] = 1
    put("swap1", s)
    s = np.zeros((P, P))
    for h in (0, 64):
        for i in range(8):
            s[h + i, h + 8 + i] = s[h + 8 + i, h + i] = 1
    put("swap2", s)
    inv = (np.float32(10000.0) ** (-np.arange(0, 64, 2, dtype=np.float32) / np.float32(64))).astype(np.float32)
    ang = (np.arange(TOK, dtype=np.float32)[None, :] * inv[:, None]).astype(np.float32)
    put("cos1", np.tile(np.cos(ang), (4, 1)))
    put("sin1", np.concatenate([-np.sin(ang), np.sin(ang)] * 2))
    q = np.arange(P)[:, None]
    k = np.arange(TOK)[None, :]
    put("mask1", np.where(k // 64 <= (q + P) // 64, 0.0, -1e30))
    put("mask0", np.where(k[:, :P] // 64 <= q // 64, 0.0, -1e30))
    put("causal1", np.where(k <= q + P, 0.0, -1e30))
    e = 16 * np.arange(16)[None, :] + 31
    put("cmp1", (e <= q + P) * 1.0)
    put("cmp0", (e <= q) * 1.0)
    put("cmo1", np.where(e <= q + P, 0.0, -1e30))
    put("cmo0", np.where(e <= q, 0.0, -1e30))
    t = np.arange(16)
    put("count", np.concatenate([1.0 / np.minimum(t + 1, w) for w in (2, 4, 8, 16)]).astype(np.float32)[None, :])
    d = np.arange(P) % 64
    inv2 = (np.float32(500000.0) ** (-np.arange(0, 16, 2, dtype=np.float32) / np.float32(16))).astype(np.float32)
    f = np.zeros((P, 4), np.float32)
    f[:, 0] = np.where(d < 16, inv2[d % 8], 0.0)
    f[:, 1] = np.where(d < 8, -1.0, np.where(d < 16, 1.0, 0.0))
    put("freq", f)
    return c


LAYER_ROWS = (("pre", KT), ("post", KT), ("qn", 3), ("kvn", 2), ("cw", CONV1 * LT), ("cb", LT),
              ("ba", LT), ("bx", LT), ("lam", LT))
ROW = {}
_at = 0
for _name, _n in LAYER_ROWS:
    ROW[_name] = _at
    _at += _n


class Walk:

    def __init__(self, eng, name, sems, steps):
        self.eng, self.name, self.sems, self.steps = eng, name, sems, steps
        self.n = defaultdict(int)
        self.loops = []

    def _loop_part(self, key, unit=1):
        total = 0
        for i, steps in self.loops:
            s = steps.get(key, 0)
            assert s % unit == 0, (self.name, key, s)
            if s:
                total = i * (s // unit) + total
        return total

    def value(self, key, more=0):
        return self._loop_part(key) + (self.n[key] + more)

    def given(self, key, k=1):
        self.n[key] += k
        return k

    def taken(self, key, k=1):
        self.n[key] += k
        return self.value(key)

    def bank(self, ring, j=0):
        return (self.n[ring] + j) % 4 + (0 if ring == "J" else 4)

    def turn(self, ring, j=0):
        return self._loop_part(ring, 4) + ((self.n[ring] + j) // 4 + 1)

    def go(self, key, k):
        self.n[key] += k

    @contextmanager
    def loop(self, label, count):
        key = f"{self.name}.{label}"
        steps = self.steps.get(key, {})
        before = dict(self.n)
        with self.eng.Fori(0, count) as i:
            self.loops.append((i, steps))
            yield i
            self.loops.pop()
        found = {k: v - before.get(k, 0) for k, v in self.n.items() if v != before.get(k, 0)}
        if steps != found:
            assert not steps, (key, steps, found)
            self.steps[key] = found
        for k, v in found.items():
            self.n[k] = before.get(k, 0) + v * count


def program(nc, steps, ins, out):
    ctx = ExitStack()
    with ctx:
        def sb(name, shape, dt=F32):
            return ctx.enter_context(nc.sbuf_tensor(name, shape, dt))

        def overlay(*plans):
            made = {}
            for number, plan in enumerate(plans):
                with ExitStack() as scope:
                    for name, shape, dt in plan:
                        t = scope.enter_context(nc.sbuf_tensor(name or f"pad{number}_{len(made)}", shape, dt))
                        made[name or f"pad{number}_{len(made)}"] = t
            return made

        def kb(n):
            return (None, [P, 256 * n], F32)

        cst = sb("cst", [P, NCONST])
        par = sb("par", [P, 7 * P])
        x = sb("x", [P, KT, TOK])
        h_hi = sb("h_hi", [P, KT, TOK], F32R)
        h_lo = sb("h_lo", [P, KT, TOK], F32R)
        m = sb("m", [P, KT, TOK])
        raw = [sb(f"raw{b}", [P, SLOT]) for b in range(2)]
        w_hi = [sb(f"w_hi{b}", [P, SLOT], F32R) for b in range(2)]
        w_lo = [sb(f"w_lo{b}", [P, SLOT], F32R) for b in range(2)]
        rs = sb("rs", [P, TOK])
        cell = sb("cell", [P, 1])
        sink = sb("sink", [P, 1])
        hf = sb("hf", [P, 2, TOK])
        decay = sb("decay", [P, L, LT])
        dt1 = sb("dt1", [P, 4, L, LT])
        sm = sb("sm", [P, 4, 16])
        ln = sb("ln", [P, 8])
        o = overlay(
            [("R", [P, LT, TOK], F32), ("I", [P, LT, TOK], F32),
             ("cqv", [P, 5, TOK], F32), ("c_hi", [P, 5, TOK], F32R), ("c_lo", [P, 5, TOK], F32R),
             ("wg", [P, 2, 2, len(PAIRS), P], F32), ("kr", [P, TOK], F32), kb(1),
             ("q", [P, HEADS, TOK], F32), ("qr", [P, 4, TOK], F32), ("kn", [P, HEADS, TOK], F32),
             ("vm", [P, TT, HEADS * VD], F32), ("krz", [P, 2, TOK], F32), ("xc", [P, LT, TOK], F32),
             ("zc", [P, LT, TOK], F32)],
            [kb(20), ("S1", [P, HEADS, TOK], F32), ("S0", [P, HEADS, P], F32), ("p0T", [P, HEADS, P], F32),
             ("p1T", [P, 2, 4, P], F32), ("zb", [P, HEADS, TOK], F32),
             ("yb_hi", [P, KT, TOK], F32R), ("yb_lo", [P, KT, TOK], F32R),
             ("vT", [P, TT, GM], F32), ("lng", [P, GM], F32), ("lnb", [P, GM], F32),
             ("uz", [P, KT, TOK], F32), ("rec", [P, 1, TOK], F32), kb(4), ("yc_hi", [P, LT, TOK], F32R), ("yc_lo", [P, LT, TOK], F32R)],
            [kb(20), ("G", [P, KT, TOK], F32), ("ya_hi", [P, KT, TOK], F32R), ("ya_lo", [P, KT, TOK], F32R)],
            [kb(20), ("ws", [P, GM_GROUPS, P], F32), ("wsT", [P, GM_GROUPS, P], F32),
             ("bs", [P, GM_GROUPS, P], F32)],
            [kb(20), ("tok_in", [P, TT, D], F32), ("rows", [P, 7, P], F32)],
            [kb(20), (None, [P, KT, TOK], F32),
             ("hp", [P, KT, 8 + TOK], F32), ("ha", [P, KT, 8 + TOK], F32), ("hb", [P, KT, 8 + TOK], F32),
             ("hu", [P, KT, TOK], F32)],
            [(None, [P, 9, TOK], F32), ("p_hi", [P, L * 2, TOK], F32R), ("p_lo", [P, L * 2, TOK], F32R), kb(3),
             (None, [P, KT, TOK], F32),
             ("y2_hi", [P, FT, TOK], F32R), ("y2_lo", [P, FT, TOK], F32R), ("ua", [P, 2, TOK], F32),
             ("ug", [P, 2, TOK], F32), ("sg", [P, 2, TOK], F32)],
            [("p_in", [P, L, TT, 256], F32), ("pf", [P, L * 2, TOK], F32)],
            [("cos2", [P, TOK], F32), ("sin2", [P, TOK], F32), ("vsw", [P, TT, 2, 256], F32), ("gt", [P, TT, 48], F32),
             ("stat", [P, 2, 4, 24], F32), ("kcz", [P, 2, 60], F32), ("vc", [P, 4, 64], F32)],
            [kb(28), ("q2", [P, KT, TOK], F32), ("kr2", [P, 4, TOK], F32), ("kz", [P, 2, 4, 2, TOK], F32),
             ("w1", [P, 2, 16, P], F32), ("cc", [P, 2, 4, TOK], F32), ("w2", [P, 2, P], F32), ("ge", [P, 4, 60], F32),
             ("kcd", [P, 60], F32), ("ang", [P, 4, TOK], F32), ("posi", [P, TOK], I32)],
            [kb(56), ("T1", [P, 2, 4, 2, TOK], F32), ("T0", [P, 2, 4, 2, P], F32), ("Tc", [P, 2, 2, 4, 16], F32),
             ("t1T", [P, 4, 4, P], F32), ("t0T", [P, 4, 2, P], F32), ("tcT", [P, 2, 4, P], F32)],
        )
        ps = [ctx.enter_context(nc.psum_tensor(f"bank{b}", [P, 512], F32)) for b in range(8)]

        sems = {n: ctx.enter_context(nc.semaphore(n)) for n in (
            ["raw_full0", "raw_full1", "hi_done", "w_split", "w_used"]
            + [f"full{b}" for b in range(8)] + [f"free{b}" for b in range(8)]
            + ["const_in", "x_in", "rows_zero", "rows_in", "par_ready", "x_ready", "sq", "mean_sq", "rstd", "hf_ready",
               "h_hi_done", "h_ready", "act_part", "dve_step", "act_step", "conv_ready", "cq_raw", "cq_f", "c_hi_done",
               "c_ready", "ms_c", "rstd_c", "kr_raw", "kr_ready", "qr_raw", "q_ready", "kv_ready", "gate_zero",
               "gate_in", "gate_used", "attn_dead", "s_ready", "p_exp", "p_ready", "pT_ready", "zb_ready", "y_f",
               "y_hi_done", "y_ready", "yc_f", "yc_hi_done", "yc_ready", "ln_sq", "ln_rstd", "m_hi_done", "v_ready", "ln_in", "ws_in", "wsT_ready", "vn_ready", "u_dead", "ln_part",
               "tanh_ready", "gates_ready", "sqrt_ask", "sqrt_done", "m_f", "m_ready", "gate_ready", "decay_part",
               "out_ready", "stored", "b_used", "table_in"] + ["p_in_done", "pf_ready", "p_hi_done", "p_ready2", "nsa_in", "pos_ready", "sin_ready", "f_f", "f_hi_done", "f_ready",
               "sg_ready", "u_f", "u_hi_done", "u_ready", "hn_ready", "cc_ready", "hid_ready", "gelu_ask", "gelu_done",
               "ge_ready", "kc_ready", "vc_ready", "k2_ready", "q2_ready", "t_ready", "t_exp", "t_done", "o_hi_done",
               "o_split", "final_ready", "nsa_zero"])}

        full, free = ([sems[f"{k}{b}"] for b in range(8)] for k in ("full", "free"))

        c = {k: cst[:, a:b] for k, (a, b) in CONST.items()}
        R, I, cqv, c_hi, c_lo, wg = o["R"], o["I"], o["cqv"], o["c_hi"], o["c_lo"], o["wg"]
        q, qr, kn, vm, kr, krz, xc, zc = o["q"], o["qr"], o["kn"], o["vm"], o["kr"], o["krz"], o["xc"], o["zc"]
        S1, S0, p0T, p1T, zb, yb_hi, yb_lo = (o[k] for k in ("S1", "S0", "p0T", "p1T", "zb", "yb_hi", "yb_lo"))
        vT, lng, lnb, uz, yc_hi, yc_lo = (o[k] for k in ("vT", "lng", "lnb", "uz", "yc_hi", "yc_lo"))
        rec = o["rec"]
        G, ya_hi, ya_lo, ws, wsT, bs = (o[k] for k in ("G", "ya_hi", "ya_lo", "ws", "wsT", "bs"))
        tok_in, rows = o["tok_in"], o["rows"]

        p_in, pf, p_hi, p_lo, hp, ha, hb, hu = (o[k] for k in ("p_in", "pf", "p_hi", "p_lo", "hp", "ha", "hb", "hu"))
        y2_hi, y2_lo, ua, ug, sg = (o[k] for k in ("y2_hi", "y2_lo", "ua", "ug", "sg"))
        cos2, sin2, vsw, gt, kcz, vc = (o[k] for k in ("cos2", "sin2", "vsw", "gt", "kcz", "vc"))
        q2, kr2, kz, w1, cc, w2, ge, kcd, ang, posi = (o[k] for k in (
            "q2", "kr2", "kz", "w1", "cc", "w2", "ge", "kcd", "ang", "posi"))
        T1, T0, Tc, t1T, t0T, tcT = (o[k] for k in ("T1", "T0", "Tc", "t1T", "t0T", "tcT"))
        stat = o["stat"]

        def mx_at(qt, n, a):
            return (qt * 4 + n) * 2 + a

        def acc(b, n=TOK):
            return ps[b][:, 0:n]

        def vec(l, name, t=0, n=1):
            return par[:, bass.ds(l * P + (ROW[name] + t), n)]

        def raw_part(b, half, query):
            if not query:
                return raw[b][:, half * HALF:(half + 1) * HALF]
            v = raw[b][:, 0:6 * QKD].rearrange("p (k h n) -> p k h n", k=3, h=2)
            return v[:, :, :, NOPE:QKD] if half else v[:, :, :, 0:NOPE]

        def split_part(t, half, query):
            if not query:
                return t[:, half * HALF:(half + 1) * HALF]
            v = t[:, 0:6 * QKD].rearrange("p (k n) -> p k n", k=3)
            return (v[:, :, 2 * NOPE:] if half else v[:, :, 0:2 * NOPE]).rearrange("p k (h n) -> p k h n", h=2)

        block = ctx.enter_context(nc.Block())
        attn_scale = 1.0 / math.sqrt(QKD)

        @block.sync
        def _(sp):
            w = Walk(sp, "sp", sems, steps)

            def load(j, dst, src):
                b = (w.n["S"] + j) % 2
                sp.wait_ge(sems["w_split"], w._loop_part("S") * 2 + (2 * (w.n["S"] + j) + 2))
                sp.dma_start(dst(raw[b]), src).then_inc(sems[f"raw_full{b}"], 16)

            def kxn(k, n):
                return lambda r: r[:, 0:k * n].rearrange("p (k n) -> p k n", k=k)

            def rows_of(t, l, r0, k, c0, n):
                return t[bass.ds(l, 1), r0:r0 + k * P, bass.ds(c0, n)].rearrange("a (k p) n -> p (a k) n", p=P)

            sp.dma_start(cst[:, :], ins["shape_constants"]).then_inc(sems["const_in"], 16)
            sp.dma_start(tok_in[:, :, :], ins["x"].rearrange("a (t p) d -> p (a t) d", p=P))\
                .then_inc(sems["x_in"], 16)
            w_in = ins["w_in"]
            with w.loop("layer", L) as l:
                with w.loop("xz", 5) as i:
                    load(0, kxn(8, SW), rows_of(w_in, l, 0, KT, i * SW + COL_XC, SW))
                    load(1, kxn(8, SW), rows_of(w_in, l, 0, KT, i * SW + COL_ZC, SW))
                    w.go("S", 2)
                for j, (c0, n) in enumerate(((COL_CQ, 256), (COL_CQ + 256, 128), (COL_CKV, 256), (COL_KR, 64))):
                    load(j, kxn(8, n), rows_of(w_in, l, 0, KT, c0, n))
                w.go("S", 4)
                for j in range(4):
                    load(j, kxn(3, 2 * QKD), rows_of(ins["mla_w_uq"], l, 0, 3, j * 2 * QKD, 2 * QKD))
                w.go("S", 4)
                for j in range(2):
                    load(j, kxn(2, 1024), rows_of(ins["mla_w_ukv"], l, 0, 2, j * 1024, 1024))
                w.go("S", 2)

                def square(label, t, c0):
                    with w.loop(label, 2) as i:
                        for j in range(2):
                            load(j, kxn(8, SW), rows_of(t, l, 0, KT, i * 2 * SW + (c0 + j * SW), SW))
                        w.go("S", 2)
                square("zb", w_in, COL_ZB)
                square("v", w_in, COL_V)
                with w.loop("uz", 4) as i:
                    load(0, kxn(8, SW), rows_of(w_in, l, 0, KT, i * SW + COL_U, SW))
                    load(1, kxn(8, SW), rows_of(w_in, l, 0, KT, i * SW + COL_ZA, SW))
                    w.go("S", 2)
                square("ga", w_in, COL_GA)
                square("a", ins["w_proj_a"], 0)
                square("gb", w_in, COL_GB)
                square("b", ins["w_proj_b"], 0)
                square("gc", w_in, COL_GC)
                with w.loop("c", 4) as i:
                    load(0, kxn(5, SW), rows_of(ins["w_proj_c"], l, 0, 5, i * SW, SW))
                    load(1, kxn(5, SW), rows_of(ins["w_proj_c"], l, 5 * P, 5, i * SW, SW))
                    w.go("S", 2)
                square("out", ins["w_out"], 0)
            dn, up = ins["ffn_down_2"], ins["ffn_up_2"]
            load(0, kxn(8, 256), ins["pool_w_2"].rearrange("a g (k p) n -> p (a g k) n", p=P))
            w.go("S", 1)

            def ffn(l):
                with w.loop("up", FT // 2) as i:
                    for j in range(2):
                        load(j, kxn(8, SW), rows_of(up, l, 0, KT, i * SW + j * FF, SW))
                    w.go("S", 2)
                with w.loop("down", 2) as i:
                    for j in range(2):
                        for k, n in enumerate((8, 8, 6)):
                            load(3 * j + k, kxn(n, SW), rows_of(dn, l, k * 8 * P, n, i * 2 * SW + j * SW, SW))
                    w.go("S", 6)
                load(0, kxn(2, D), rows_of(ins["ple_proj_2"], l, 0, 2, 0, D))
                w.go("S", 1)
                with w.loop("ple", 2) as i:
                    for j in range(2):
                        load(j, kxn(8, SW), rows_of(ins["ple_gate_2"], l, 0, KT, i * 2 * SW + j * SW, SW))
                    w.go("S", 2)
            ffn(0)
            for j in range(6):
                load(j, kxn(8, SW), ins["w_kv_2"][:, j * SW:(j + 1) * SW].rearrange("(k p) n -> p k n", p=P))
            w.go("S", 6)
            load(0, kxn(8, 48), rows_of(ins["w_in_b_2"], 0, 0, KT, D, 48))
            w.go("S", 1)
            for label, t in (("q2", ins["w_in_b_2"]), ("o2", ins["w_out_b_2"])):
                with w.loop(label, 2) as i:
                    for j in range(2):
                        load(j, kxn(8, SW), rows_of(t, 0, 0, KT, i * 2 * SW + j * SW, SW))
                    w.go("S", 2)
            ffn(1)
            sp.wait_ge(sems["out_ready"], 1)
            sp.dma_start(out.rearrange("a (t p) d -> p (a t) d", p=P),
                         x[:, :, :].rearrange("p (t a) n -> p t (a n)", t=TT)).then_inc(sems["stored"], 16)
            sp.wait_ge(sems["stored"], 16)

        def credit(pool):
            pool.sem_inc(sems["w_split"], 4)
            pool.sem_inc(sems["b_used"], 1)
            pool.sem_inc(sems["f_ready"], 2)
            for b in range(8):
                pool.sem_inc(sems[f"free{b}"], 1)

        @block.gpsimd
        def _(pool):
            w = Walk(pool, "pool", sems, steps)
            pool.memset(cell[:, :], 0.0)
            pool.memset(rows[:, :, :], 0.0).then_inc(sems["rows_zero"], w.given("rows_zero"))
            pool.wait_ge(sems["rows_zero"], w.value("rows_zero"))
            count = 0
            for l in range(L):
                for name, n in LAYER_ROWS:
                    key = {"pre": "pre_norm_g", "post": "post_norm_g", "qn": "mla_q_norm_g", "kvn": "mla_kv_norm_g",
                           "cw": "lru_conv_w", "cb": "lru_conv_b", "ba": "lru_b_a", "bx": "lru_b_x",
                           "lam": "lru_lambda"}[name]
                    src = ins[key][l]
                    src = (src.rearrange("j (t p) -> (j t) p", p=P) if name == "cw"
                           else src.rearrange("(t p) -> t p", p=P))
                    pool.dma_start(rows[ROW[name]:ROW[name] + n, l, :], src).then_inc(sems["rows_in"], 16)
                    count += 1
            def row(first, n, src):
                pool.dma_start(rows[first % P:first % P + n, first // P, :], src).then_inc(sems["rows_in"], 16)
            for name, n, src in (("mix", L * KT, ins["norm_mix_2"].rearrange("l (t p) -> (l t) p", p=P)),
                                 ("scale", KT, ins["pool_scale_2"].rearrange("l (t p) -> (l t) p", p=P)),
                                 ("kv", KT, ins["norm_kv_2"].rearrange("(t p) -> t p", p=P)),
                                 ("ffn", L * KT, ins["norm_ffn_2"].rearrange("l (t p) -> (l t) p", p=P)),
                                 ("ple", L * KT, ins["norm_ple_2"].rearrange("l (t p) -> (l t) p", p=P)),
                                 ("final", KT, ins["norm_final_2"].rearrange("(t p) -> t p", p=P)),
                                 ("posk", 16, ins["cmp_pos_k_2"].rearrange("(t a) d -> t (a d)", a=2)),
                                 ("posv", 16, ins["cmp_pos_v_2"].rearrange("(t a) d -> t (a d)", a=2))):
                row(ROW2[name], n, src)
                count += 1
            for l in range(L):
                cw = ins["ffn_conv_2"][l].rearrange("j (t p) -> (j t) p", p=P)
                row(conv_row(l, 0), 4 * FT, cw[0:4 * FT, :])
                row(conv_row(l, 2), 2 * FT, cw[4 * FT:6 * FT, :])
                row(conv_row(l, 3), 2 * FT, ins["ffn_conv_b_2"][l].rearrange("(t p) -> t p", p=P))
                count += 3
            assert count == ROW_LOADS, count
            credit(pool)
            with w.loop("layer", L) as l:
                w.n["b_used"] += 1
                pool.wait_ge(sems["b_used"], w.value("b_used"))
                pool.tensor_tensor(cell[:, :], cell[:, :], cell[:, :], ALU.add)
                pool.memset(wg[:, :, :, :, :], 0.0).then_inc(sems["gate_zero"], w.given("gate_zero"))
                pool.wait_ge(sems["gate_zero"], w.value("gate_zero"))
                for g, t in enumerate((ins["lru_w_a"], ins["lru_w_x"])):
                    for pair, r, rb, nr, cc, cb, ncol, b in gate_pieces():
                        src = t[bass.ds(l, 1), b:b + 9:8, rb:rb + nr, cb:cb + ncol].rearrange("a h i j -> i (a h) j")
                        pool.dma_start(wg[r:r + nr, g, :, pair, cc:cc + ncol], src).then_inc(sems["gate_in"], 16)
                pool.wait_ge(sems["attn_dead"], w.taken("attn_dead"))
                for dst, key in ((lng, "gm_ln_g"), (lnb, "gm_ln_b")):
                    pool.dma_start(dst[:, :], ins[key][bass.ds(l, 1), :].rearrange("a n -> (a n)").partition_broadcast(P))\
                        .then_inc(sems["ln_in"], 16)
                pool.dma_start(ws[:, :, :], ins["gm_ws"][bass.ds(l, 1)].rearrange("a g i j -> i (a g) j"))\
                    .then_inc(sems["ws_in"], 16)
                pool.dma_start(bs[:, :, :].rearrange("p g j -> p (g j)"),
                               ins["gm_bs"][bass.ds(l, 1)].rearrange("a g j -> (a g j)").partition_broadcast(P))\
                    .then_inc(sems["ws_in"], 16)
            pool.wait_ge(sems["x_ready"], KT * (1 + L))
            pool.dma_start(p_in[:, :, :, :], ins["p_2"].rearrange("l a (t p) n -> p l (a t) n", p=P))\
                .then_inc(sems["p_in_done"], 16)
            pool.wait_ge(sems["x_ready"], KT * (1 + L + 3))
            pool.memset(w2[:, :, :], 0.0)
            pool.memset(kz[:, :, :, :, :], 0.0).then_inc(sems["nsa_zero"], w.given("nsa_zero"))
            pool.wait_ge(sems["nsa_zero"], w.value("nsa_zero"))
            pool.dma_start(posi[:, :], ins["positions_2"].rearrange("a n -> (a n)").partition_broadcast(P))\
                .then_inc(sems["nsa_in"], 16)
            for n, (a, b) in enumerate((("cmp_w1_k_2", "cmp_w2_k_2"), ("cmp_w1_v_2", "cmp_w2_v_2"))):
                pool.dma_start(w1[:, n, :, :], ins[a].rearrange("(k p) n -> p k n", p=P)).then_inc(sems["nsa_in"], 16)
                for half in range(2 - n):
                    pool.dma_start(w2[:, n, half * 64:half * 64 + 64], ins[b]).then_inc(sems["nsa_in"], 16)

        @block.tensor
        def _(pe):
            w = Walk(pe, "pe", sems, steps)

            def wait_half(j, half):
                pe.wait_ge(sems["w_split"], w._loop_part("S") * 2 + (2 * (w.n["S"] + j) + half + 5))

            def three(out_, lh, ll, rh, rl, start, stop):
                pe.matmul(out_, lh, rh, start=start, stop=False)
                pe.matmul(out_, lh, rl, start=False, stop=False)
                return pe.matmul(out_, ll, rh, start=False, stop=stop)

            def features(j, job, k_tiles, row, cols, act, k0=0, start=True, stop=True,
                         whole=False, ready=None, tiles=KT):
                b = (w.n["S"] + j) % 2
                hi, lo = act
                banks = [w.bank("J", job + t) for t in range(len(cols))]
                if start:
                    for t, bank in enumerate(banks):
                        pe.wait_ge(free[bank], w.turn("J", job + t))
                wait_half(j, int(whole))
                for k in range(k_tiles):
                    if ready:
                        pe.wait_ge(sems[ready], w.value(ready, k0 + k + 1 - tiles))
                    for t, (c0, width) in enumerate(cols):
                        a = k * row + c0
                        if a + width > HALF and not whole:
                            wait_half(j, 1)
                            whole = True
                        mm = three(ps[banks[t]][0:width, 0:TOK], w_hi[b][:, a:a + width], w_lo[b][:, a:a + width],
                                   hi[:, k0 + k, :], lo[:, k0 + k, :],
                                   start and k == 0, stop and k == k_tiles - 1)
                        if k == k_tiles - 1 and stop:
                            mm.then_inc(sems[f"full{banks[t]}"], 1)
                if not stop:
                    mm.then_inc(sems["w_used"], w.given("w_used"))

            def tokens(j, job, k_tiles, act, cols, width):
                b = (w.n["S"] + j) % 2
                banks = [w.bank("J", job + t) for t in range(TT)]
                for t, bank in enumerate(banks):
                    pe.wait_ge(free[bank], w.turn("J", job + t))
                wait_half(j, 1)
                for k in range(k_tiles):
                    for t in range(TT):
                        hi, lo = (a[:, k, t * P:(t + 1) * P] for a in act)
                        mm = three(ps[banks[t]][:, 0:width], hi, lo, cols(k, w_hi[b]), cols(k, w_lo[b]),
                                   k == 0, k == k_tiles - 1)
                        if k == k_tiles - 1:
                            mm.then_inc(sems[f"full{banks[t]}"], 1)

            def side(j=0):
                b = w.bank("K", j)
                pe.wait_ge(free[b], w.turn("K", j))
                return b

            def filled(ins, b):
                ins.then_inc(sems[f"full{b}"], 1)
                w.go("K", 1)

            def norm_sum(sq, n, takes):
                b = side()
                for t in range(n):
                    if t % (n // takes) == 0:
                        pe.wait_ge(sems["sq"], w.taken("sq"))
                    mm = pe.matmul(acc(b), c["ones"], sq[:, t, :], start=(t == 0), stop=(t == n - 1))
                filled(mm, b)

            def transposes(blocks):
                b = side()
                for n, src in enumerate(blocks):
                    mm = pe.transpose(ps[b][:, n * P:(n + 1) * P], src, c["ident"])
                filled(mm, b)

            def keys_values(j, job, act):
                b = (w.n["S"] + j) % 2
                hi, lo = (t[b][:, :].rearrange("p (k h n) -> p k h n", k=2, h=4) for t in (w_hi, w_lo))
                wait_half(j, 1)
                for t in range(4):
                    bank = w.bank("J", job + t)
                    pe.wait_ge(free[bank], w.turn("J", job + t))
                    for k in range(2):
                        mm = three(acc(bank), hi[:, k, t, 0:NOPE], lo[:, k, t, 0:NOPE],
                                   act[0][:, k, :], act[1][:, k, :], k == 0, k == 1)
                    mm.then_inc(sems[f"full{bank}"], 1)
                for t in range(TT):
                    bank = w.bank("J", job + 4 + t)
                    pe.wait_ge(free[bank], w.turn("J", job + 4 + t))
                    for k in range(2):
                        mm = three(ps[bank][:, :], act[0][:, k, t * P:(t + 1) * P], act[1][:, k, t * P:(t + 1) * P],
                                   hi[:, k, :, NOPE:2 * P], lo[:, k, :, NOPE:2 * P], k == 0, k == 1)
                    mm.then_inc(sems[f"full{bank}"], 1)

            h = (h_hi, h_lo)
            TWO = [(0, P), (P, P)]

            pe.wait_ge(sems["const_in"], 16)
            pe.wait_ge(sems["x_in"], 16)
            for u in range(KT // 2):
                transposes([tok_in[:, t, (2 * u + f) * P:(2 * u + f + 1) * P] for f in range(2) for t in range(TT)])
            pe.wait_ge(sems["rows_in"], 16 * ROW_LOADS)
            for u in range(4):
                transposes([rows[:, r, :] for r in range(2 * u, min(2 * u + 2, 7))])
            with w.loop("layer", L) as l:
                norm_sum(G, KT, 2)
                w.go("h_ready", KT)
                with w.loop("xz", 5):
                    features(0, 0, KT, SW, TWO, h, ready="h_ready")
                    features(1, 2, KT, SW, TWO, h)
                    w.go("S", 2), w.go("J", 4)
                features(0, 0, KT, 256, TWO, h)
                features(1, 2, KT, P, [(0, P)], h)
                features(2, 3, KT, 256, TWO, h)
                features(3, 5, KT, 64, [(0, 64)], h)
                for job, t0, n in ((6, 0, 3), (7, 3, 2)):
                    b = w.bank("J", job)
                    pe.wait_ge(free[b], w.turn("J", job))
                    pe.wait_ge(sems["cq_raw"], w.taken("cq_raw", n))
                    for t in range(n):
                        mm = pe.matmul(acc(b), c["ones"], m[:, t0 + t, :], start=(t == 0), stop=(t == n - 1))
                    mm.then_inc(sems[f"full{b}"], 1)
                pe.wait_ge(sems["conv_ready"], w.taken("conv_ready", LT))
                pe.wait_ge(sems["gate_in"], w.taken("gate_in", 16 * 2 * len(gate_pieces())))
                for t in range(LT):
                    rep, o_ = t // 5, t % 5
                    near = [(n, i_) for n, (oo, i_) in enumerate(PAIRS) if oo == o_]
                    for g in range(2):
                        b = side()
                        for n, (pair, i_) in enumerate(near):
                            mm = pe.matmul(acc(b), wg[:, g, rep, pair, :], xc[:, 5 * rep + i_, :],
                                           start=(n == 0), stop=(n == len(near) - 1))
                        filled(mm, b)
                b = side()
                pe.wait_ge(free[w.bank("J", 5)], w.turn("J", 5) + 1)
                filled(pe.matmul(acc(b), c["swap1"], kr[:, :], start=True, stop=True), b)
                w.go("S", 4), w.go("J", 8)
                pe.wait_ge(sems["c_ready"], w.taken("c_ready", 5))
                for j in range(4):
                    features(j, 3 * j, 3, 2 * QKD, [(0, P), (P, P), (2 * P, P)], (c_hi, c_lo), whole=True)
                for j in range(4):
                    b = side()
                    pe.wait_ge(free[w.bank("J", 3 * j + 2)], w.turn("J", 3 * j + 2) + 1)
                    filled(pe.matmul(acc(b), c["swap1"], qr[:, j, :], start=True, stop=True), b)
                w.go("S", 4), w.go("J", 12)
                ckv = (c_hi[:, 3:5, :], c_lo[:, 3:5, :])
                for j in range(2):
                    keys_values(j, 6 * j, ckv)
                w.go("S", 2), w.go("J", 12)
                pe.wait_ge(sems["q_ready"], w.taken("q_ready", 6))
                for j in range(1, 5):
                    pe.wait_ge(free[w.bank("J", -j)], w.turn("J", -j) + 1)
                for j in range(4):
                    b = side()
                    for n in range(2):
                        hd = 2 * j + n
                        pe.matmul(ps[b][:, n * TOK:(n + 1) * TOK], q[:, hd, P:TOK], kn[:, hd, :], start=True, stop=False)
                        mm = pe.matmul(ps[b][:, n * TOK:(n + 1) * TOK], qr[:, j, P:TOK],
                                       krz[:, n, :], start=False, stop=True)
                    filled(mm, b)
                for j in range(2):
                    b = side()
                    for n in range(4):
                        hd = 4 * j + n
                        pe.matmul(ps[b][:, n * P:(n + 1) * P], q[:, hd, 0:P], kn[:, hd, 0:P], start=True, stop=False)
                        mm = pe.matmul(ps[b][:, n * P:(n + 1) * P], qr[:, hd // 2, 0:P],
                                       krz[:, hd % 2, 0:P], start=False, stop=True)
                    filled(mm, b)

                def square(label, act, ready=None):
                    with w.loop(label, 2):
                        for j in range(2):
                            features(j, 2 * j, KT, SW, TWO, act, ready=None if j else ready)
                        w.go("S", 2), w.go("J", 4)
                square("zb", h)
                pe.wait_ge(sems["p_ready"], w.taken("p_ready"))
                for j in range(2):
                    transposes([S0[:, 4 * j + n, :] for n in range(4)])
                pe.wait_ge(sems["p_ready"], w.taken("p_ready"))

                def turn_pair(j):
                    transposes([S1[:, 2 * j + n, k * P:(k + 1) * P] for n in range(2) for k in range(TT)])

                def pv(j, behind):
                    pe.wait_ge(free[w.bank("K", -behind)], w.turn("K", -behind) + 1)
                    for n in range(2):
                        hd = 2 * j + n
                        b = side()
                        v_ = [vm[:, t, hd * VD:(hd + 1) * VD] for t in range(TT)]
                        pe.matmul(ps[b][:, 0:P], v_[0], p0T[:, hd, :], start=True, stop=True)
                        for k in range(TT):
                            mm = pe.matmul(ps[b][:, P:TOK], v_[k], p1T[:, j % 2, 2 * n + k, :],
                                           start=(k == 0), stop=(k == TT - 1))
                        filled(mm, b)
                turn_pair(0)
                turn_pair(1)
                pe.wait_ge(free[w.bank("K", -3)], w.turn("K", -3) + 1)
                pe.wait_ge(free[w.bank("K", -4)], w.turn("K", -4) + 1)
                pv(0, 2)
                turn_pair(2)
                pv(1, 4)
                turn_pair(3)
                pv(2, 4)
                pv(3, 3)
                pe.drain().then_inc(sems["attn_dead"], w.given("attn_dead"))
                with w.loop("v", 2):
                    for j in range(2):
                        tokens(j, 2 * j, KT, h, lambda k, t: t[:, k * SW:(k + 1) * SW], SW)
                    w.go("S", 2), w.go("J", 4)
                pe.wait_ge(sems["ws_in"], w.taken("ws_in", 32))
                transposes([ws[:, g, :] for g in range(GM_GROUPS)])
                with w.loop("uz", 4):
                    features(0, 0, KT, SW, TWO, h)
                    features(1, 2, KT, SW, TWO, h)
                    w.go("S", 2), w.go("J", 4)
                pe.wait_ge(sems["wsT_ready"], w.taken("wsT_ready"))
                pe.wait_ge(sems["vn_ready"], w.taken("vn_ready"))
                for t in range(KT):
                    b = side()
                    for n in range(TT):
                        mm = pe.matmul(ps[b][:, n * P:(n + 1) * P], vT[:, n, t * P:(t + 1) * P],
                                       wsT[:, t * GM_GROUPS // KT, :], start=True, stop=True)
                    filled(mm, b)
                square("ga", h)
                w.go("y_ready", 2 * KT)
                square("a", (ya_hi, ya_lo), "y_ready")
                square("gb", h)
                square("b", (yb_hi, yb_lo))
                pe.drain().then_inc(sems["b_used"], w.given("b_used"))
                square("gc", h)
                w.go("yc_ready", LT)
                with w.loop("c", 2):
                    for j in range(2):
                        ready = None if j else "yc_ready"
                        features(2 * j, 2 * j, 5, SW, TWO, (yc_hi, yc_lo), stop=False, ready=ready, tiles=LT)
                        features(2 * j + 1, 2 * j, 5, SW, TWO, (yc_hi, yc_lo), k0=5, start=False, ready=ready, tiles=LT)
                    w.go("S", 4), w.go("J", 4)
                w.go("m_ready", KT)
                square("out", h, "m_ready")
                norm_sum(G, KT, KT)
            w.go("f_ready", 2)
            norm_sum(G, KT, 2)
            pe.wait_ge(sems["p_in_done"], 16)
            for l in range(L):
                transposes([p_in[:, l, t, f * P:(f + 1) * P] for f in range(2) for t in range(TT)])
            pe.wait_ge(sems["u_ready"], w.taken("u_ready", KT))
            for g in range(4):
                features(0, 2 * g, 2, SW, [(g * 512, P), (g * 512 + P, P)], h, k0=2 * g, whole=True)
            w.go("S", 1), w.go("J", 8)

            def ffn(l):
                norm_sum(G, KT, KT if l else 2)
                w.go("h_ready", KT)
                with w.loop("up", FT // 2):
                    features(0, 0, KT, SW, TWO, h, ready="h_ready")
                    features(1, 2, KT, SW, TWO, h)
                    w.go("S", 2), w.go("J", 4)
                w.go("f_ready", FT)
                with w.loop("down", 2):
                    for j in range(2):
                        for k, n in enumerate((8, 8, 6)):
                            features(3 * j + k, 2 * j, n, SW, TWO, (y2_hi, y2_lo), k0=8 * k, start=k == 0, stop=k == 2,
                                     ready=None if j else "f_ready", tiles=FT)
                    w.go("S", 6), w.go("J", 4)
                norm_sum(G, KT, KT)
                pe.wait_ge(sems["p_ready2"], w.taken("p_ready2"))
                for n in range(2):
                    features(0, 4 * n, 2, D, [((4 * n + t) * P, P) for t in range(4)],
                             (p_hi[:, 2 * l:2 * l + 2, :], p_lo[:, 2 * l:2 * l + 2, :]), whole=True)
                w.go("S", 1), w.go("J", 8)
                w.go("h_ready", KT)
                square("ple", h, "h_ready")
            ffn(0)
            norm_sum(G, KT, 2)
            w.go("h_ready", KT)
            whole_slot = lambda k, t: t[:, k * SW:(k + 1) * SW]
            for j in range(6):
                if j in (3, 5):
                    tokens(j, 2 * j, KT, h, whole_slot, SW)
                else:
                    features(j, 2 * j, KT, SW, TWO, h, ready=None if j else "h_ready")
            w.go("S", 6), w.go("J", 12)
            for t in range(4):
                b = side()
                pe.wait_ge(free[w.bank("J", (-8, -7, -4, -3)[t])], w.turn("J", (-8, -7, -4, -3)[t]) + 1)
                filled(pe.matmul(acc(b), c["swap2"], kr2[:, t, :], start=True, stop=True), b)
            pe.wait_ge(sems["cc_ready"], w.taken("cc_ready"))
            pe.wait_ge(sems["nsa_in"], 96)
            b = side()
            for n in range(2):
                for k in range(16):
                    pe.matmul(ps[b][:, 64 * n:64 * n + 60].rearrange("p (g n) -> p g n", g=4), w1[:, n, k, :],
                              cc[:, n, :, 2 * k:2 * k + 225:16], start=(k == 0), stop=(k == 15))
                for k in range(16):
                    mm = pe.matmul(ps[b][:, 128 + n:129 + n], w1[:, n, k, :],
                                   par[:, ROW2["posv" if n else "posk"] + k:ROW2["posv" if n else "posk"] + k + 1],
                                   start=(k == 0), stop=(k == 15))
            filled(mm, b)
            pe.wait_ge(sems["h_ready"], w.taken("h_ready", KT))
            tokens(0, 0, KT, h, lambda k, t: t[:, k * 48:(k + 1) * 48], 48)
            w.go("S", 1), w.go("J", 2)
            pe.wait_ge(sems["ge_ready"], w.taken("ge_ready"))
            b = side()
            filled(pe.matmul(ps[b][:, 0:60], w2[:, 0, :], ge[:, 2, :], start=True, stop=True), b)
            b = side()
            for g in range(NG):
                mm = pe.matmul(ps[b][0:NCMP, g * HD:(g + 1) * HD], ge[:, 3, g * NCMP:(g + 1) * NCMP], w2[:, 1, 0:HD],
                               start=True, stop=True)
            filled(mm, b)
            b = side()
            pe.wait_ge(sems["kc_ready"], w.taken("kc_ready"))
            filled(pe.matmul(ps[b][:, 0:60], c["swap2"], kcd[:, :], start=True, stop=True), b)
            square("q2", h)
            for t in range(KT):
                b = side()
                if t == 0:
                    for j in range(1, 5):
                        pe.wait_ge(free[w.bank("J", -j)], w.turn("J", -j) + 1)
                filled(pe.matmul(acc(b), c["swap2"], q2[:, t, :], start=True, stop=True), b)
            pe.wait_ge(sems["k2_ready"], w.taken("k2_ready"))
            pe.wait_ge(sems["vc_ready"], w.taken("vc_ready"))

            def scores2(g):
                pe.wait_ge(sems["q2_ready"], w.taken("q2_ready", 2))
                b = side()
                for qt in range(TT):
                    for n in range(4):
                        t = 2 * g + n // 2
                        at = (qt * 4 + n) * 16
                        mm = pe.matmul(ps[b][:, at:at + NCMP], q2[:, t, qt * P:(qt + 1) * P],
                                       kcz[:, n % 2, g * NCMP:(g + 1) * NCMP], start=True, stop=True)
                filled(mm, b)
                for u in range(2):
                    b = side()
                    for n in range(2):
                        mm = pe.matmul(ps[b][:, n * TOK:(n + 1) * TOK].rearrange("p (a k) -> p a k", a=2),
                                       q2[:, 2 * g + u, 0:P], kz[:, n, g, :, 0:P], start=True, stop=True)
                    filled(mm, b)
                for n in range(4):
                    b = side()
                    filled(pe.matmul(ps[b][:, :], q2[:, 2 * g + n // 2, P:TOK],
                                     kz[:, n % 2, g, :, :].rearrange("p a k -> p (a k)"), start=True, stop=True), b)

            def values2(g):
                r = g % 2
                pe.wait_ge(sems["t_done"], w.taken("t_done"))
                for qt in range(TT):
                    b = side()
                    for n in range(4):
                        mm = pe.transpose(ps[b][0:16, n * P:(n + 1) * P], Tc[:, r, qt, n, :], c["ident"])
                    filled(mm, b)
                for u in range(2):
                    transposes([T0[:, r, 2 * u + n, a, :] for n in range(2) for a in range(2)])
                for n in range(4):
                    transposes([T1[:, r, n, a, k * P:(k + 1) * P] for a in range(2) for k in range(TT)])
                for j in range(1, 9):
                    pe.wait_ge(free[w.bank("K", -j)], w.turn("K", -j) + 1) if j <= 4 else None
                for qt in range(TT):
                    b = side()
                    for n in range(4):
                        o_ = ps[b][:, n * HD:(n + 1) * HD]
                        pe.matmul(o_, tcT[0:NCMP, qt, n, :], vc[0:NCMP, g, :], start=True, stop=False)
                        for a in range(2):
                            for k in range(qt + 1):
                                pt = t0T[:, n, a, :] if qt == 0 else t1T[:, n, 2 * a + k, :]
                                mm = pe.matmul(o_, pt, vsw[:, k, a, g * HD:(g + 1) * HD], start=False,
                                               stop=(a == 1 and k == qt))
                    filled(mm, b)
            scores2(0)
            for g in range(NG):
                if g + 1 < NG:
                    scores2(g + 1)
                values2(g)
            pe.wait_ge(free[w.bank("K", -1)], w.turn("K", -1) + 1)
            pe.wait_ge(free[w.bank("K", -2)], w.turn("K", -2) + 1)
            mt = m[:, :, :].rearrange("p (t a) n -> p t (a n)", t=TT)
            for u in range(KT // 2):
                transposes([mt[:, t, (2 * u + f) * P:(2 * u + f + 1) * P] for f in range(2) for t in range(TT)])
            w.go("o_split", KT)
            square("o2", h, "o_split")
            ffn(1)
            norm_sum(G, KT, 2)
            pe.wait_ge(sems["final_ready"], w.taken("final_ready"))
            for t in range(TT):
                for u in range(2):
                    transposes([m[:, 4 * u + f, t * P:(t + 1) * P] for f in range(4)])


        @block.scalar
        def _(act):
            w = Walk(act, "act", sems, steps)

            def hi(j, half, after=None, query=False):
                b = (w.n["S"] + j) % 2
                if half == 0:
                    act.wait_ge(sems[f"raw_full{b}"], w._loop_part("S") * 8 + 16 * ((w.n["S"] + j + 2) // 2 + 1))
                    if after is None:
                        act.wait_ge(sems["w_used"], w.taken("w_used"))
                    else:
                        act.wait_ge(full[w.bank("J", after)], w.turn("J", after))
                act.copy(split_part(w_hi[b], half, query), raw_part(b, half, query)).then_inc(sems["hi_done"], 1)

            def evac(ring, j, dst, func=None, scale=1.0, bias=0.0, width=TOK, rows_=P, src=None):
                b = w.bank(ring, j)
                act.wait_ge(full[b], w.turn(ring, j))
                ins_ = act.activation(dst, ps[b][0:rows_, 0:width] if src is None else src(ps[b]),
                                      func or ACT.Identity, bias=bias, scale=scale)
                ins_.then_inc(free[w.bank(ring, j)], 1)

            def first_of(ring, j, dst, func, bias=0.0, scale=1.0):
                b = w.bank(ring, j)
                act.wait_ge(full[b], w.turn(ring, j))
                act.activation(dst, acc(b), func, bias=bias, scale=scale)\
                    .then_inc(sems["act_part"], w.given("act_part"))

            def norm(src, squares_ready=False):
                if not squares_ready:
                    for half in range(2):
                        act.wait_ge(sems["x_ready"], w.taken("x_ready", KT // 2))
                        part = slice(half * KT // 2, (half + 1) * KT // 2)
                        act.activation(G[:, part, :], src[:, part, :], ACT.Square).then_inc(sems["sq"], w.given("sq"))
                act.wait_ge(sems["mean_sq"], w.taken("mean_sq"))
                act.activation(rs[:, :], rs[:, :], ACT.Sqrt).then_inc(sems["rstd"], w.given("rstd"))

            def split_h():
                for t in range(KT):
                    act.wait_ge(sems["hf_ready"], w.taken("hf_ready"))
                    act.copy(h_hi[:, t, :], hf[:, t % 2, :]).then_inc(sems["h_hi_done"], w.given("h_hi_done"))

            def table(func):
                act.wait_ge(sems["table_in"], w.value("table_in"))
                act.activation(sink[:, :], c["ones"][:, 0:1], func).then_inc(sems["table_in"], w.given("table_in"))

            act.wait_ge(sems["const_in"], 16)
            act.copy(sink[:, :], c["ones"][:, 0:1]).then_inc(sems["table_in"], w.given("table_in"))
            for b in range(2):
                act.wait_ge(sems[f"raw_full{b}"], 16)
                for half in range(2):
                    part = slice(half * HALF, (half + 1) * HALF)
                    act.copy(w_hi[b][:, part], raw[b][:, part]).then_inc(sems["hi_done"], 1)
            w.go("K", 8)
            act.wait_ge(sems["decay_part"], w.taken("decay_part"))
            act.activation(dt1[:, 1, :, :], dt1[:, 0, :, :], ACT.Exp).then_inc(sems["act_part"], w.given("act_part"))

            def dyn(i, k, n):
                return bass.ds(i * k + n, 1)

            def root(i, tile0):
                t = dyn(i, 1, tile0)
                act.wait_ge(sems["sqrt_ask"], w.taken("sqrt_ask"))
                act.activation(R[:, t, :], R[:, t, :], ACT.Sqrt).then_inc(sems["sqrt_done"], w.given("sqrt_done"))

            def high_yc(i, tile0):
                t = dyn(i, 1, tile0)
                act.wait_ge(sems["yc_f"], w.taken("yc_f"))
                act.copy(yc_hi[:, t, :], R[:, t, :]).then_inc(sems["yc_hi_done"], w.given("yc_hi_done"))

            with w.loop("layer", L) as l:
                norm(x)
                split_h()
                w.go("K", 1)
                with w.loop("xz", 5) as i:
                    table(ACT.Sigmoid)
                    for n in range(2):
                        hi(0, n, after=1)
                        first_of("J", n, xc[:, dyn(i, 2, n), :], ACT.Identity,
                                 bias=par[:, bass.ds(l * P + (i * 2 + (ROW["cb"] + n)), 1)],
                                 scale=par[:, bass.ds(l * P + (i * 2 + (ROW["cw"] + 3 * LT + n)), 1)])
                    for n in range(2):
                        hi(1, n, after=3)
                        first_of("J", 2 + n, zc[:, dyn(i, 2, n), :], ACT.Sigmoid)
                    w.go("S", 2), w.go("J", 4)
                job = 0
                for j, nt in enumerate((2, 1, 2)):
                    for n in range(2):
                        hi(j, n, after=job + nt - 1, query=j == 2)
                    for n in range(nt):
                        b = w.bank("J", job)
                        act.wait_ge(full[b], w.turn("J", job))
                        act.activation(m[:, job, :], acc(b), ACT.Square).then_inc(sems["cq_raw"], w.given("cq_raw"))
                        evac("J", job, cqv[:, job, :])
                        job += 1
                hi(3, 0, after=5, query=True)
                hi(3, 1, query=True)
                b = w.bank("J", 5)
                act.wait_ge(full[b], w.turn("J", 5))
                act.activation(kr[0:64, :], ps[b][0:64, 0:TOK], ACT.Identity)
                evac("J", 5, kr[64:128, :], rows_=64)
                act.wait_ge(sems["ms_c"], w.taken("ms_c"))
                act.activation(hf[:, :, :], hf[:, :, :], ACT.Sqrt).then_inc(sems["rstd_c"], w.given("rstd_c"))
                for t in range(5):
                    act.wait_ge(sems["cq_f"], w.taken("cq_f"))
                    act.copy(c_hi[:, t, :], cqv[:, t, :]).then_inc(sems["c_hi_done"], w.given("c_hi_done"))
                for t in range(LT):
                    for g, (dst, name) in enumerate(((R, "ba"), (I, "bx"))):
                        b = w.bank("K", 2 * t + g)
                        act.wait_ge(full[b], w.turn("K", 2 * t + g))
                        ins_ = act.activation(dst[:, t, :], acc(b), ACT.Sigmoid, bias=vec(l, name, t))
                        ins_.then_inc(free[w.bank("K", 2 * t + g)], 1)
                    act.wait_ge(free[w.bank("K", 2 * t)], w.turn("K", 2 * t) + 1)
                    act.activation(R[:, t, :], R[:, t, :], ACT.Tanh,
                                          scale=decay[:, bass.ds(l, 1), t])\
                                              .then_inc(sems["tanh_ready"], w.given("tanh_ready"))
                w.go("K", 20 + 1 + 4)
                w.go("S", 4), w.go("J", 8)
                for j in range(4):
                    hi(j, 0, after=3 * j + 2, query=j < 2)
                    evac("J", 3 * j, q[:, 2 * j, :])
                    evac("J", 3 * j + 1, q[:, 2 * j + 1, :])
                    hi(j, 1, query=j < 2)
                    evac("J", 3 * j + 2, qr[:, j, :])
                w.go("S", 4), w.go("J", 12)
                for j in range(2):
                    for n in range(4):
                        evac("J", 6 * j + n, kn[:, 4 * j + n, :])
                    hi(j, 0, after=6 * j + 5)
                    hi(j, 1)
                w.go("S", 2), w.go("J", 12)
                w.go("K", 6)

                def zb_slot(i, j):
                    for n in range(2):
                        hi(j, n, after=2 * j + 1)
                        first_of("J", 2 * j + n, zb[:, dyn(i, 4, 2 * j + n), :], ACT.Sigmoid)
                for first, S, col in ((True, S0, 8), (False, S1, 0)):
                    act.wait_ge(sems["s_ready"], w.taken("s_ready"))
                    for hd in range(HEADS):
                        ins_ = act.activation(S[:, hd, :], S[:, hd, :], ACT.Exp, bias=sm[:, 1, col + hd:col + hd + 1],
                                              accum_out=sm[:, 2, col + hd:col + hd + 1])
                    ins_.then_inc(sems["p_exp"], w.given("p_exp"))
                with w.loop("zb", 2) as i:
                    table(ACT.Sigmoid)
                    for j in range(2):
                        zb_slot(i, j)
                    w.go("S", 2), w.go("J", 4)
                for j in range(2):
                    evac("K", j, p0T[:, 4 * j:4 * j + 4, :].rearrange("p a b -> p (a b)"), width=512)
                w.go("K", 2)

                def turned(k, j, behind=None):
                    if behind is not None:
                        act.wait_ge(full[w.bank("K", behind)], w.turn("K", behind))
                    evac("K", k, p1T[:, j % 2, :, :].rearrange("p a b -> p (a b)"), width=512)

                def y_tile(k, t, hi_part):
                    act.wait_ge(free[w.bank("K", k)], w.turn("K", k) + 1)
                    act.copy(hi_part[:, t, :], hf[:, t % 2, :]).then_inc(sems["y_hi_done"], w.given("y_hi_done"))
                turned(0, 0)
                turned(1, 1)
                y_tile(2, 0, yb_hi), y_tile(3, 1, yb_hi)
                turned(4, 2, behind=3)
                y_tile(5, 2, yb_hi), y_tile(6, 3, yb_hi)
                turned(7, 3, behind=6)
                for n in range(4):
                    y_tile(8 + n, 4 + n, yb_hi)
                w.go("K", 12)
                with w.loop("v", 2) as i:
                    for j in range(2):
                        hi(j, 0, after=2 * j + 1)
                        evac("J", 2 * j, vT[:, 0, bass.ds(i * 512 + j * SW, SW)])
                        hi(j, 1, after=2 * j + 1)
                        evac("J", 2 * j + 1, vT[:, 1, bass.ds(i * 512 + j * SW, SW)])
                    w.go("S", 2), w.go("J", 4)
                mf = m[:, :, :].rearrange("p (a b) n -> p a (b n)", a=2)
                act.wait_ge(sems["ln_part"], w.taken("ln_part"))
                for t in range(TT):
                    ins_ = act.activation(mf[:, t, :], vT[:, t, :], ACT.Square, accum_out=ln[:, 4 + t:5 + t])
                ins_.then_inc(sems["ln_sq"], w.given("ln_sq"))
                act.wait_ge(sems["ln_part"], w.taken("ln_part"))
                act.activation(ln[:, 6:8], ln[:, 6:8], ACT.Sqrt).then_inc(sems["ln_rstd"], w.given("ln_rstd"))
                w.go("K", 1)
                with w.loop("uz", 4) as i:
                    for n in range(2):
                        hi(0, n, after=1)
                        evac("J", n, uz[:, dyn(i, 2, n), :])
                    root(i, 0)
                    for n in range(2):
                        hi(1, n, after=3)
                        first_of("J", 2 + n, m[:, dyn(i, 2, n), :], ACT.Sigmoid)
                    high_yc(i, 0)
                    w.go("S", 2), w.go("J", 4)
                for t in range(KT):
                    act.wait_ge(sems["y_f"], w.taken("y_f"))
                    act.copy(ya_hi[:, t, :], hf[:, t % 2, :]).then_inc(sems["y_hi_done"], w.given("y_hi_done"))
                w.go("K", 8)

                def gate(label, tile0):
                    with w.loop(label, 2) as i:
                        table(ACT.Sigmoid)
                        for j in range(2):
                            for n in range(2):
                                hi(j, n, after=2 * j + 1)
                                evac("J", 2 * j + n, G[:, dyn(i, 4, 2 * j + n), :], ACT.Sigmoid)
                            if j == 0 and tile0 is not None:
                                root(i, tile0)
                        if tile0 is not None:
                            high_yc(i, tile0)
                        w.go("S", 2), w.go("J", 4)

                def idle(label, tile0=None):
                    with w.loop(label, 2) as i:
                        for j in range(2):
                            for n in range(2):
                                hi(j, n, after=2 * j + 1)
                            if j == 0 and tile0 is not None:
                                root(i, tile0)
                        if tile0 is not None:
                            high_yc(i, tile0)
                        w.go("S", 2), w.go("J", 4)

                def evacuated_all():
                    for j in range(1, 5):
                        act.wait_ge(free[w.bank("J", -j)], w.turn("J", -j) + 1)
                gate("ga", 4)
                idle("a", 6)
                evacuated_all()
                gate("gb", 8)
                idle("b")
                evacuated_all()
                gate("gc", None)
                with w.loop("c", 2) as i:
                    for j in range(2):
                        hi(2 * j, 0)
                        hi(2 * j, 1)
                        hi(2 * j + 1, 0, after=2 * j + 1)
                        hi(2 * j + 1, 1)
                        for n in range(2):
                            act.wait_ge(sems["m_f"], w.taken("m_f"))
                            t = dyn(i, 4, 2 * j + n)
                            act.copy(h_hi[:, t, :], m[:, t, :]).then_inc(sems["m_hi_done"], w.given("m_hi_done"))
                    w.go("S", 4), w.go("J", 4)
                evacuated_all()
                with w.loop("out", 2) as i:
                    for j in range(2):
                        for n in range(2):
                            hi(j, n, after=2 * j + 1)
                            t = dyn(i, 4, 2 * j + n)
                            b = w.bank("J", 2 * j + n)
                            act.wait_ge(full[b], w.turn("J", 2 * j + n))
                            act.activation(G[:, t, :], acc(b), ACT.Square).then_inc(sems["sq"], w.given("sq"))
                            evac("J", 2 * j + n, m[:, t, :])
                    w.go("S", 2), w.go("J", 4)
                norm(None, squares_ready=True)
                w.go("K", 1)
            def col(r, n=1):
                return par[:, bass.ds(r, n)]

            norm(x)
            w.go("K", 1)
            for t in range(KT):
                act.wait_ge(sems["u_f"], w.taken("u_f"))
                act.copy(h_hi[:, t, :], hu[:, t, :]).then_inc(sems["u_hi_done"], w.given("u_hi_done"))
            for l in range(L):
                act.wait_ge(sems["pf_ready"], w.taken("pf_ready"))
                for f in range(2):
                    ins_ = act.copy(p_hi[:, 2 * l + f, :], pf[:, 2 * l + f, :])
                ins_.then_inc(sems["p_hi_done"], w.given("p_hi_done"))
            w.go("K", 2)
            hi(0, 0, after=7)
            hi(0, 1)
            w.go("S", 1), w.go("J", 8)

            def squares(i, j):
                for n in range(2):
                    act.wait_ge(free[w.bank("J", 2 * j + n)], w.turn("J", 2 * j + n) + 1)
                    t = dyn(i, 4, 2 * j + n)
                    act.activation(G[:, t, :], x[:, t, :], ACT.Square).then_inc(sems["sq"], w.given("sq"))

            def ffn(l):
                norm(x, squares_ready=l == 1)
                w.go("K", 1)
                split_h()
                with w.loop("up", FT // 2) as i:
                    table(ACT.Sigmoid)
                    for s, (dst, c0) in enumerate(((ua, 0), (ug, FT))):
                        for n in range(2):
                            hi(s, n, after=2 * s + 1)
                            if s == n == 0:
                                act.wait_ge(sems["f_ready"], w.taken("f_ready", 2))
                            first_of("J", 2 * s + n, dst[:, n, :], ACT.Identity,
                                     bias=col(i * 2 + (conv_row(l, 3) + c0 + n)),
                                     scale=col(i * 2 + (conv_row(l, 2) + c0 + n)))
                    for n in range(2):
                        act.wait_ge(free[w.bank("J", 2 + n)], w.turn("J", 2 + n) + 1)
                        act.activation(sg[:, n, :], ug[:, n, :], ACT.Sigmoid)\
                            .then_inc(sems["sg_ready"], w.given("sg_ready"))
                    for n in range(2):
                        act.wait_ge(sems["f_f"], w.taken("f_f"))
                        act.copy(y2_hi[:, dyn(i, 2, n), :], ua[:, n:n + 1, :])\
                            .then_inc(sems["f_hi_done"], w.given("f_hi_done"))
                    w.go("S", 2), w.go("J", 4)
                with w.loop("down", 2) as i:
                    for j in range(2):
                        for k in range(3):
                            hi(3 * j + k, 0, after=2 * j + 1 if k == 2 else None)
                            hi(3 * j + k, 1)
                        squares(i, j)
                    w.go("S", 6), w.go("J", 4)
                w.go("x_ready", KT)
                norm(x, squares_ready=True)
                w.go("K", 1)
                for t in range(KT):
                    evac("J", t, m[:, t, :])
                hi(0, 0, after=7)
                hi(0, 1)
                split_h()
                w.go("S", 1), w.go("J", 8)

                def ple(i, ahead):
                    if ahead:
                        table(ACT.Sigmoid)
                    for j in range(2):
                        for n in range(2):
                            if ahead:
                                hi(j, n, after=2 * j + 1)
                            evac("J", 2 * j + n, G[:, dyn(i, 4, 2 * j + n), :], ACT.Sigmoid)
                    w.go("S", 2), w.go("J", 4)
                if l + 1 < L:
                    with w.loop("ple", 2) as i:
                        ple(i, True)
                else:
                    ple(0, True)
                    ple(1, False)
            ffn(0)
            norm(x)
            w.go("K", 1)
            split_h()
            for j in range(6):
                if j == 1:
                    act.wait_ge(sems["pos_ready"], w.taken("pos_ready"))
                    act.activation(sin2[:, :], ang[:, 1, :], ACT.Sin)
                    act.activation(cos2[:, :], ang[:, 2, :], ACT.Sin)\
                        .then_inc(sems["sin_ready"], w.given("sin_ready"))
                for n in range(2):
                    hi(j, n, after=2 * j + 1)
                    b = w.bank("J", 2 * j + n)
                    act.wait_ge(full[b], w.turn("J", 2 * j + n))
                    if j < 2:
                        for g_ in range(2):
                            src = ps[b][64 * g_:64 * g_ + 64, 0:TOK]
                            act.activation(cc[0:64, j, 2 * n + g_, :], src, ACT.Identity)
                            ins_ = act.activation(cc[64:P, j, 2 * n + g_, 0:TOK - 1], src[:, 1:TOK], ACT.Identity)
                        ins_.then_inc(free[w.bank("J", 2 * j + n)], 1)
                    elif j in (2, 4):
                        evac("J", 2 * j + n, kr2[:, j - 2 + n, :])
                    else:
                        evac("J", 2 * j + n, vsw[:, n, (j - 3) // 2, :])
                if j == 1:
                    act.drain().then_inc(sems["cc_ready"], w.given("cc_ready"))
            w.go("S", 6), w.go("J", 12)
            w.go("K", 5)
            split_h()
            act.wait_ge(sems["gelu_ask"], w.taken("gelu_ask"))
            act.activation(ge[:, 2:4, :], ge[:, 2:4, :], ACT.Tanh, scale=math.sqrt(2 / math.pi))\
                .then_inc(sems["gelu_done"], w.given("gelu_done"))
            hi(0, 0, after=1)
            for t in range(TT):
                evac("J", t, gt[:, t, :], ACT.Sigmoid, width=48)
            hi(0, 1)
            w.go("S", 1), w.go("J", 2)
            evac("K", 0, kcd[:, :], width=60)
            b = w.bank("K", 1)
            act.wait_ge(full[b], w.turn("K", 1))
            act.activation(vc[0:NCMP, :, :].rearrange("p g n -> p (g n)"), ps[b][0:NCMP, 0:256], ACT.Identity)\
                .then_inc(free[w.bank("K", 1)], 1)
            act.wait_ge(free[w.bank("K", 1)], w.turn("K", 1) + 1)
            act.drain().then_inc(sems["kc_ready"], w.given("kc_ready"))
            w.go("K", 3)
            with w.loop("q2", 2) as i:
                for j in range(2):
                    for n in range(2):
                        hi(j, n, after=2 * j + 1)
                        evac("J", 2 * j + n, q2[:, dyn(i, 4, 2 * j + n), :])
                w.go("S", 2), w.go("J", 4)
            w.go("K", KT)

            def exps2(g):
                r = g % 2
                act.wait_ge(sems["t_ready"], w.taken("t_ready"))
                act.activation(Tc[:, r, :, :, :], Tc[:, r, :, :, :], ACT.Exp)
                for qt, T in enumerate((T0, T1)):
                    for n in range(4):
                        for a in range(2):
                            at = mx_at(qt, n, a)
                            ins_ = act.activation(T[:, r, n, a, :], T[:, r, n, a, :], ACT.Exp,
                                                  bias=stat[:, r, 1, at:at + 1], accum_out=stat[:, r, 2, at:at + 1])
                ins_.then_inc(sems["t_exp"], w.given("t_exp"))
                w.go("K", 7)

            def turned2(g):
                for qt in range(TT):
                    b = w.bank("K", qt)
                    act.wait_ge(full[b], w.turn("K", qt))
                    act.activation(tcT[0:16, qt, :, :].rearrange("p a n -> p (a n)"), ps[b][0:16, :],
                                           ACT.Identity).then_inc(free[w.bank("K", qt)], 1)
                for u in range(2):
                    evac("K", 2 + u, t0T[:, 2 * u:2 * u + 2, :, :].rearrange("p a b n -> p (a b n)"), width=512)
                for n in range(4):
                    evac("K", 4 + n, t1T[:, n, :, :].rearrange("p b n -> p (b n)"), width=512)
                mt = m[:, :, :].rearrange("p (t a) n -> p t (a n)", t=TT)
                for qt in range(TT):
                    evac("K", 8 + qt, mt[:, qt, g * 256:(g + 1) * 256], width=256)
                w.go("K", 10)
            exps2(0)
            for g in range(NG):
                if g + 1 < NG:
                    exps2(g + 1)
                turned2(g)
            for u in range(KT // 2):
                b = w.bank("K", u)
                act.wait_ge(full[b], w.turn("K", u))
                act.copy(h_hi[:, 2 * u:2 * u + 2, :].rearrange("p a n -> p (a n)"), ps[b][:, :])\
                    .then_inc(sems["o_hi_done"], w.given("o_hi_done"))
            w.go("K", 4)
            with w.loop("o2", 2) as i:
                for j in range(2):
                    for n in range(2):
                        hi(j, n, after=2 * j + 1)
                    squares(i, j)
                w.go("S", 2), w.go("J", 4)
            w.go("x_ready", KT)
            ffn(1)
            norm(x)
            w.go("K", 1)

        @block.vector
        def _(dve):
            w = Walk(dve, "dve", sems, steps)

            def lo(j, half, query=False):
                b = (w.n["S"] + j) % 2
                dve.wait_ge(sems["hi_done"], w._loop_part("S") * 2 + (2 * (w.n["S"] + j + 2) + half + 1))
                dve.tensor_tensor(split_part(w_lo[b], half, query), raw_part(b, half, query),
                                  split_part(w_hi[b], half, query).bitcast(F32), ALU.subtract)\
                    .then_inc(sems["w_split"], 1)

            def recip_mean(dst, src, n, ring=None, j=0):
                ins_ = dve.tensor_scalar(dst, src, 1.0 / n, EPS, ALU.mult, ALU.add)
                if ring is None:
                    ins_.then_inc(sems["dve_step"], w.given("dve_step"))
                    dve.wait_ge(sems["dve_step"], w.value("dve_step"))
                else:
                    ins_.then_inc(free[w.bank(ring, j)], 1)
                    dve.wait_ge(free[w.bank(ring, j)], w.turn(ring, j) + 1)
                return dve.reciprocal(dst, dst)

            def total(n=D):
                b = w.bank("K")
                dve.wait_ge(full[b], w.turn("K"))
                recip_mean(rs[:, :], acc(b), n, "K").then_inc(sems["mean_sq"], w.given("mean_sq"))
                w.go("K", 1)
                dve.wait_ge(sems["rstd"], w.taken("rstd"))

            def norm_h(src, gain):
                total()
                h_tiles(src, gain)

            def h_tiles(src, gain):
                def full(t):
                    dve.scalar_tensor_tensor(hf[:, t % 2, :], src[:, t, :], gain(t), rs[:, :],
                                                    ALU.mult, ALU.mult)\
                                                        .then_inc(sems["hf_ready"], w.given("hf_ready"))
                full(0)
                for t in range(KT):
                    if t + 1 < KT:
                        if t:
                            dve.wait_ge(sems["h_ready"], w.value("h_ready"))
                        full(t + 1)
                    dve.wait_ge(sems["h_hi_done"], w.taken("h_hi_done"))
                    dve.tensor_tensor(h_lo[:, t, :], hf[:, t % 2, :], h_hi[:, t, :].bitcast(F32),
                                             ALU.subtract).then_inc(sems["h_ready"], w.given("h_ready"))

            def dyn(i, k, n):
                return bass.ds(i * k + n, 1)

            for b in range(2):
                for half in range(2):
                    part = slice(half * HALF, (half + 1) * HALF)
                    dve.wait_ge(sems["hi_done"], 2 * b + half + 1)
                    dve.tensor_tensor(w_lo[b][:, part], raw[b][:, part], w_hi[b][:, part].bitcast(F32), ALU.subtract)\
                        .then_inc(sems["w_split"], 1)
            for u in range(KT // 2):
                b = w.bank("K", u)
                dve.wait_ge(full[b], w.turn("K", u))
                dve.tensor_copy(x[:, 2 * u:2 * u + 2, :].rearrange("p a b -> p (a b)"), ps[b][:, :])\
                    .then_inc(free[w.bank("K", u)], 1)
            dve.drain().then_inc(sems["x_ready"], w.given("x_ready", KT))
            for u in range(4):
                n = 2 * P if u < 3 else P
                b = w.bank("K", 4 + u)
                dve.wait_ge(full[b], w.turn("K", 4 + u))
                dve.tensor_copy(par[:, 2 * u * P:2 * u * P + n], ps[b][:, 0:n]).then_inc(free[w.bank("K", 4 + u)], 1)
                dve.wait_ge(free[w.bank("K", 4 + u)], w.turn("K", 4 + u) + 1)
            w.go("K", 8)
            lam = par[:, 0:2 * P].rearrange("p (l n) -> p l n", l=2)[:, :, ROW["lam"]:ROW["lam"] + LT]
            dve.tensor_scalar(dt1[:, 0, :, :], lam, -1.0, None, ALU.mult)\
                .then_inc(sems["dve_step"], w.given("dve_step"))
            dve.wait_ge(sems["dve_step"], w.value("dve_step"))
            dve.tensor_tensor(dt1[:, 0, :, :], dt1[:, 0, :, :], lam, ALU.min)\
                .then_inc(sems["dve_step"], w.given("dve_step"))
            dve.wait_ge(sems["dve_step"], w.value("dve_step"))
            dve.tensor_scalar(dt1[:, 3, :, :], lam, -1.0, 0.0, ALU.mult, ALU.max)\
                .then_inc(sems["decay_part"], w.given("decay_part"))
            dve.wait_ge(sems["act_part"], w.taken("act_part"))
            e_, z_, z2, s_ = (dt1[:, n, :, :] for n in (1, 0, 2, 1))
            dve.tensor_scalar(z_, e_, 2.0, None, ALU.add).then_inc(sems["dve_step"], w.given("dve_step"))
            dve.wait_ge(sems["dve_step"], w.value("dve_step"))
            dve.reciprocal(z_, z_).then_inc(sems["dve_step"], w.given("dve_step"))
            dve.wait_ge(sems["dve_step"], w.value("dve_step"))
            dve.tensor_tensor(z_, z_, e_, ALU.mult).then_inc(sems["dve_step"], w.given("dve_step"))
            dve.wait_ge(sems["dve_step"], w.value("dve_step"))
            dve.tensor_tensor(z2, z_, z_, ALU.mult).then_inc(sems["dve_step"], w.given("dve_step"))
            dve.wait_ge(sems["dve_step"], w.value("dve_step"))
            dve.tensor_scalar(s_, z2, 1.0 / 19, 1.0 / 17, ALU.mult, ALU.add)\
                .then_inc(sems["dve_step"], w.given("dve_step"))
            dve.wait_ge(sems["dve_step"], w.value("dve_step"))
            for k in range(15, 0, -2):
                dve.tensor_tensor(s_, s_, z2, ALU.mult).then_inc(sems["dve_step"], w.given("dve_step"))
                dve.wait_ge(sems["dve_step"], w.value("dve_step"))
                dve.tensor_scalar(s_, s_, 1.0 / k, None, ALU.add).then_inc(sems["dve_step"], w.given("dve_step"))
                dve.wait_ge(sems["dve_step"], w.value("dve_step"))
            dve.scalar_tensor_tensor(s_, s_, 2.0, z_, ALU.mult, ALU.mult)\
                .then_inc(sems["dve_step"], w.given("dve_step"))
            dve.wait_ge(sems["dve_step"], w.value("dve_step"))
            dve.tensor_tensor(s_, s_, dt1[:, 3, :, :], ALU.add).then_inc(sems["dve_step"], w.given("dve_step"))
            dve.wait_ge(sems["dve_step"], w.value("dve_step"))
            dve.tensor_scalar(decay[:, :, :], s_, 4.0, None, ALU.mult).then_inc(sems["dve_step"], w.given("dve_step"))
            dve.wait_ge(sems["dve_step"], w.value("dve_step"))

            def begin(t):
                dve.wait_ge(sems["tanh_ready"], w.taken("tanh_ready"))
                dve.tensor_tensor(xc[:, t, :], xc[:, t, :], I[:, t, :], ALU.mult)
                ins_ = dve.tensor_scalar(rec[:, :, :], R[:, t, :], 1.0, None, ALU.add)
                ins_.then_inc(sems["sqrt_ask"], w.given("sqrt_ask"))
                w.n["sqrt_own"] += 1
                dve.wait_ge(sems["sqrt_ask"], w.value("sqrt_own"))
                dve.reciprocal(rec[:, :, :], rec[:, :, :]).then_inc(sems["dve_step"], w.given("dve_step"))
                dve.wait_ge(sems["dve_step"], w.value("dve_step"))

            def finish(t):
                dve.wait_ge(sems["sqrt_done"], w.taken("sqrt_done"))
                dve.scalar_tensor_tensor(R[:, t, :], R[:, t, :], 2.0, rec[:, :, :], ALU.mult, ALU.mult)\
                    .then_inc(sems["dve_step"], w.given("dve_step"))
                dve.wait_ge(sems["dve_step"], w.value("dve_step"))
                dve.tensor_tensor(xc[:, t, :], R[:, t, :], xc[:, t, :], ALU.mult)
                dve.tensor_scalar(I[:, t, :], rec[:, :, :], 2.0, -1.0, ALU.mult, ALU.add)\
                    .then_inc(sems["dve_step"], w.given("dve_step"))
                dve.wait_ge(sems["dve_step"], w.value("dve_step"))
                dve.tensor_tensor_scan(R[:, t, :].rearrange("p a n -> p (a n)"),
                                            I[:, t, :].rearrange("p a n -> p (a n)"),
                                            xc[:, t, :].rearrange("p a n -> p (a n)"), 0.0, ALU.mult, ALU.add)\
                                                .then_inc(sems["dve_step"], w.given("dve_step"))
                dve.wait_ge(sems["dve_step"], w.value("dve_step"))
                dve.tensor_tensor(R[:, t, :], R[:, t, :], zc[:, t, :], ALU.mult)\
                    .then_inc(sems["yc_f"], w.given("yc_f"))

            def last(t):
                dve.wait_ge(sems["yc_hi_done"], w.taken("yc_hi_done"))
                dve.tensor_tensor(yc_lo[:, t, :], R[:, t, :], yc_hi[:, t, :].bitcast(F32), ALU.subtract)\
                    .then_inc(sems["yc_ready"], w.given("yc_ready"))

            with w.loop("layer", L) as l:
                norm_h(x, lambda t: vec(l, "pre", t))
                with w.loop("xz", 5) as i:
                    for n in range(2):
                        lo(0, n)
                    for n in range(2):
                        dve.wait_ge(sems["act_part"], w.taken("act_part"))
                        b = w.bank("J", n)
                        t = dyn(i, 2, n)
                        for d in range(1, CONV1):
                            ins_ = dve.scalar_tensor_tensor(
                                xc[:, t, d:TOK], ps[b][:, 0:TOK - d].rearrange("p (a n) -> p a n", a=1),
                                par[:, bass.ds(l * P + (i * 2 + (ROW["cw"] + (3 - d) * LT + n)), 1)],
                                xc[:, t, d:TOK], ALU.mult, ALU.add)
                            if d < 3:
                                ins_.then_inc(sems["dve_step"], w.given("dve_step"))
                                dve.wait_ge(sems["dve_step"], w.value("dve_step"))
                        ins_.then_inc(free[w.bank("J", n)], 1)
                    for n in range(2):
                        lo(1, n)
                    for n in range(2):
                        dve.wait_ge(sems["act_part"], w.taken("act_part"))
                        b = w.bank("J", 2 + n)
                        t = dyn(i, 2, n)
                        dve.tensor_tensor(zc[:, t, :], zc[:, t, :], acc(b).rearrange("p (a n) -> p a n", a=1),
                                                  ALU.mult).then_inc(free[w.bank("J", 2 + n)], 1)
                    w.go("S", 2), w.go("J", 4)
                dve.drain().then_inc(sems["conv_ready"], LT)
                for j in range(4):
                    lo(j, 0, j >= 2), lo(j, 1, j >= 2)
                for k, n in enumerate((QR, KVR)):
                    b = w.bank("J", 6 + k)
                    dve.wait_ge(full[b], w.turn("J", 6 + k))
                    ins_ = recip_mean(hf[:, k, :], acc(b), n, "J", 6 + k)
                ins_.then_inc(sems["ms_c"], w.given("ms_c"))
                dve.wait_ge(sems["rstd_c"], w.taken("rstd_c"))
                for t in range(5):
                    dve.scalar_tensor_tensor(cqv[:, t, :], cqv[:, t, :],
                                                    vec(l, "qn", t) if t < 3 else vec(l, "kvn", t - 3),
                                                    hf[:, t // 3, :], ALU.mult, ALU.mult)\
                                                        .then_inc(sems["cq_f"], w.given("cq_f"))
                for t in range(5):
                    dve.wait_ge(sems["c_hi_done"], w.taken("c_hi_done"))
                    dve.tensor_tensor(c_lo[:, t, :], cqv[:, t, :], c_hi[:, t, :].bitcast(F32), ALU.subtract)\
                        .then_inc(sems["c_ready"], w.given("c_ready"))
                w.go("S", 4), w.go("J", 8)
                w.go("K", 20)

                def rotate(t, k, first=False):
                    if not first:
                        dve.wait_ge(sems["q_ready"], w.value("q_ready"))
                    b = w.bank("K")
                    dve.wait_ge(full[b], w.turn("K"))
                    ins_ = dve.tensor_tensor(hf[:, k % 2, :], acc(b), c["sin1"], ALU.mult)
                    ins_.then_inc(free[w.bank("K")], 1)
                    dve.wait_ge(free[w.bank("K")], w.turn("K") + 1)
                    dve.tensor_tensor(t, t, c["cos1"], ALU.mult).then_inc(sems["dve_step"], w.given("dve_step"))
                    dve.wait_ge(sems["dve_step"], w.value("dve_step"))
                    dve.tensor_tensor(t, t, hf[:, k % 2, :], ALU.add).then_inc(sems["q_ready"], w.given("q_ready"))
                    w.go("K", 1)
                rotate(kr[:, :], 0, first=True)
                dve.wait_ge(sems["q_ready"], w.value("q_ready"))
                dve.memset(krz[0:64, 1, :], 0.0)
                dve.memset(krz[64:P, 0, :], 0.0)
                dve.tensor_copy(krz[0:64, 0, :], kr[0:64, :])
                dve.tensor_copy(krz[64:P, 1, :], kr[64:P, :]).then_inc(sems["q_ready"], w.given("q_ready"))
                for j in range(4):
                    lo(j, 0, j < 2), lo(j, 1, j < 2)
                for j in range(4):
                    rotate(qr[:, j, :], j)
                w.go("S", 4), w.go("J", 12)
                for j in range(2):
                    for t in range(TT):
                        b = w.bank("J", 6 * j + 4 + t)
                        dve.wait_ge(full[b], w.turn("J", 6 * j + 4 + t))
                        dve.tensor_copy(vm[:, t, j * 512:(j + 1) * 512], ps[b][:, :])\
                            .then_inc(free[w.bank("J", 6 * j + 4 + t)], 1)
                    lo(j, 0), lo(j, 1)
                w.go("S", 2), w.go("J", 12)
                for j in range(4):
                    b = w.bank("K", j)
                    dve.wait_ge(full[b], w.turn("K", j))
                    ins_ = dve.scalar_tensor_tensor(S1[:, 2 * j:2 * j + 2, :],
                                                    ps[b][:, :].rearrange("p (a n) -> p a n", a=2), attn_scale,
                                                    c["mask1"].unsqueeze(1).to_broadcast([P, 2, TOK]), ALU.mult, ALU.add)
                    ins_.then_inc(free[w.bank("K", j)], 1)
                for j in range(2):
                    b = w.bank("K", 4 + j)
                    dve.wait_ge(full[b], w.turn("K", 4 + j))
                    ins_ = dve.scalar_tensor_tensor(S0[:, 4 * j:4 * j + 4, :],
                                                    ps[b][:, :].rearrange("p (a n) -> p a n", a=4), attn_scale,
                                                    c["mask0"].unsqueeze(1).to_broadcast([P, 4, P]), ALU.mult, ALU.add)
                    ins_.then_inc(free[w.bank("K", 4 + j)], 1)
                for j in range(6):
                    dve.wait_ge(free[w.bank("K", j)], w.turn("K", j) + 1)
                w.go("K", 6)
                for S, col in ((S0, 8), (S1, 0)):
                    dve.tensor_reduce(sm[:, 0, col:col + 8], S[:, :, :], AX.X, ALU.max)\
                        .then_inc(sems["dve_step"], w.given("dve_step"))
                    dve.wait_ge(sems["dve_step"], w.value("dve_step"))
                    dve.tensor_scalar(sm[:, 1, col:col + 8], sm[:, 0, col:col + 8], -1.0, None, ALU.mult)\
                        .then_inc(sems["s_ready"], w.given("s_ready"))
                for S, col, n in ((S0, 8, P), (S1, 0, TOK)):
                    dve.wait_ge(sems["p_exp"], w.taken("p_exp"))
                    dve.reciprocal(sm[:, 3, col:col + 8], sm[:, 2, col:col + 8])\
                        .then_inc(sems["dve_step"], w.given("dve_step"))
                    dve.wait_ge(sems["dve_step"], w.value("dve_step"))
                    dve.tensor_tensor(S[:, :, :], S[:, :, :],
                                             sm[:, 3, col:col + 8].unsqueeze(2).to_broadcast([P, 8, n]), ALU.mult)\
                                                 .then_inc(sems["p_ready"], w.given("p_ready"))
                with w.loop("zb", 2) as i:
                    for j in range(2):
                        for n in range(2):
                            lo(j, n)
                            dve.wait_ge(sems["act_part"], w.taken("act_part"))
                            t = dyn(i, 4, 2 * j + n)
                            b = w.bank("J", 2 * j + n)
                            dve.tensor_tensor(zb[:, t, :], zb[:, t, :],
                                                      acc(b).rearrange("p (a n) -> p a n", a=1), ALU.mult)\
                                                          .then_inc(free[w.bank("J", 2 * j + n)], 1)
                    w.go("S", 2), w.go("J", 4)
                for j in range(1, 5):
                    dve.wait_ge(free[w.bank("J", -j)], w.turn("J", -j) + 1)
                w.go("K", 2)

                def low_y(t, lo_part, hi_part):
                    dve.wait_ge(sems["y_hi_done"], w.taken("y_hi_done"))
                    dve.tensor_tensor(lo_part[:, t, :], hf[:, t % 2, :], hi_part[:, t, :].bitcast(F32),
                                             ALU.subtract).then_inc(sems["y_ready"], w.given("y_ready"))

                def yb_tile(k, t):
                    if t > 1:
                        dve.wait_ge(sems["y_ready"], w.value("y_ready"))
                    b = w.bank("K", k)
                    dve.wait_ge(full[b], w.turn("K", k))
                    dve.tensor_tensor(hf[:, t % 2, :], acc(b), zb[:, t, :], ALU.mult)\
                        .then_inc(free[w.bank("K", k)], 1)
                order = (2, 3, 5, 6, 8, 9, 10, 11)
                yb_tile(order[0], 0)
                for t in range(HEADS):
                    if t + 1 < HEADS:
                        yb_tile(order[t + 1], t + 1)
                    low_y(t, yb_lo, yb_hi)
                w.go("K", 12)
                with w.loop("v", 2) as i:
                    for j in range(2):
                        lo(j, 0), lo(j, 1)
                    w.go("S", 2), w.go("J", 4)
                for j in range(1, 5):
                    dve.wait_ge(free[w.bank("J", -j)], w.turn("J", -j) + 1)
                dve.tensor_reduce(ln[:, 0:2], vT[:, :, :], AX.X, ALU.add)\
                    .then_inc(sems["dve_step"], w.given("dve_step"))
                dve.wait_ge(sems["dve_step"], w.value("dve_step"))
                dve.tensor_scalar(ln[:, 2:4], ln[:, 0:2], -1.0 / GM, None, ALU.mult)\
                    .then_inc(sems["dve_step"], w.given("dve_step"))
                dve.wait_ge(sems["dve_step"], w.value("dve_step"))
                dve.tensor_scalar(vT[:, 0, :], vT[:, 0, :], ln[:, 2:3], None, ALU.add)
                dve.tensor_scalar(vT[:, 1, :], vT[:, 1, :], ln[:, 3:4], None, ALU.add)\
                    .then_inc(sems["ln_part"], w.given("ln_part"))
                dve.wait_ge(sems["ln_sq"], w.taken("ln_sq"))
                dve.tensor_scalar(ln[:, 6:8], ln[:, 4:6], 1.0 / GM, EPS, ALU.mult, ALU.add)\
                    .then_inc(sems["dve_step"], w.given("dve_step"))
                dve.wait_ge(sems["dve_step"], w.value("dve_step"))
                dve.reciprocal(ln[:, 6:8], ln[:, 6:8]).then_inc(sems["ln_part"], w.given("ln_part"))
                dve.wait_ge(sems["ln_rstd"], w.taken("ln_rstd"))
                b = w.bank("K")
                dve.wait_ge(full[b], w.turn("K"))
                ins_ = dve.tensor_copy(wsT[:, :, :].rearrange("p g n -> p (g n)"), ps[b][:, :])
                ins_.then_inc(free[w.bank("K")], 1)
                dve.wait_ge(free[w.bank("K")], w.turn("K") + 1)
                dve.memset(wsT[64:P, :, 0:64], 0.0).then_inc(sems["wsT_ready"], w.given("wsT_ready"))
                w.go("K", 1)
                with w.loop("uz", 4) as i:
                    begin(dyn(i, 1, 0))
                    for n in range(2):
                        lo(0, n)
                    finish(dyn(i, 1, 0))
                    for n in range(2):
                        lo(1, n)
                    for n in range(2):
                        dve.wait_ge(sems["act_part"], w.taken("act_part"))
                        t = dyn(i, 2, n)
                        b = w.bank("J", 2 + n)
                        dve.tensor_tensor(m[:, t, :], m[:, t, :], acc(b).rearrange("p (a n) -> p a n", a=1),
                                                  ALU.mult).then_inc(free[w.bank("J", 2 + n)], 1)
                    for n in range(2):
                        t = dyn(i, 2, n)
                        dve.wait_ge(free[w.bank("J", 2 + n)], w.turn("J", 2 + n) + 1)
                        dve.tensor_tensor(uz[:, t, :], uz[:, t, :], m[:, t, :], ALU.mult)
                    last(dyn(i, 1, 0))
                    w.go("S", 2), w.go("J", 4)
                dve.wait_ge(sems["ln_in"], w.taken("ln_in", 32))
                for t in range(TT):
                    dve.scalar_tensor_tensor(vT[:, t, :], vT[:, t, :], ln[:, 6 + t:7 + t], lng[:, :],
                                                  ALU.mult, ALU.mult).then_inc(sems["dve_step"], w.given("dve_step"))
                    dve.wait_ge(sems["dve_step"], w.value("dve_step"))
                for t in range(TT):
                    ins_ = dve.tensor_tensor(vT[:, t, :], vT[:, t, :], lnb[:, :], ALU.add)
                ins_.then_inc(sems["vn_ready"], w.given("vn_ready"))
                dve.wait_ge(sems["ws_in"], w.taken("ws_in", 32))
                dve.wait_ge(sems["yc_ready"], w.value("yc_ready"))

                def ya_tile(t):
                    dve.wait_ge(sems["y_ready"], w.value("y_ready"))
                    b = w.bank("K", t)
                    dve.wait_ge(full[b], w.turn("K", t))
                    ins_ = dve.tensor_tensor(hf[:, t % 2, :].rearrange("p (a n) -> p a n", a=2),
                                             acc(b).rearrange("p (a n) -> p a n", a=2),
                                             bs[:, t * GM_GROUPS // KT, :].unsqueeze(1).to_broadcast([P, 2, P]), ALU.add)
                    ins_.then_inc(free[w.bank("K", t)], 1)
                    dve.wait_ge(free[w.bank("K", t)], w.turn("K", t) + 1)
                    dve.tensor_tensor(hf[:, t % 2, :], hf[:, t % 2, :], uz[:, t, :], ALU.mult)\
                        .then_inc(sems["y_f"], w.given("y_f"))
                ya_tile(0)
                for t in range(KT):
                    if t + 1 < KT:
                        ya_tile(t + 1)
                    low_y(t, ya_lo, ya_hi)
                w.go("K", 8)

                def with_recurrence(label, tile0, evacuate):
                    with w.loop(label, 2) as i:
                        if tile0 is not None:
                            begin(dyn(i, 1, tile0))
                        for j in range(2):
                            for n in range(2):
                                lo(j, n)
                            if j == 0 and tile0 is not None:
                                finish(dyn(i, 1, tile0))
                            for n in range(2):
                                evacuate(i, 2 * j + n)
                        if tile0 is not None:
                            last(dyn(i, 1, tile0))
                        w.go("S", 2), w.go("J", 4)

                def three_d(b):
                    return acc(b).rearrange("p (a n) -> p a n", a=1)

                def set_merged(i, k):
                    b = w.bank("J", k)
                    dve.wait_ge(full[b], w.turn("J", k))
                    t = dyn(i, 4, k)
                    dve.tensor_tensor(m[:, t, :], G[:, t, :], three_d(b), ALU.mult).then_inc(free[w.bank("J", k)], 1)

                def add_merged(i, k, j=None):
                    j = k if j is None else j
                    b = w.bank("J", j)
                    dve.wait_ge(full[b], w.turn("J", j))
                    t = dyn(i, 4, k)
                    dve.tensor_tensor(hf[:, k % 2:k % 2 + 1, :], G[:, t, :], three_d(b), ALU.mult)\
                        .then_inc(free[w.bank("J", j)], 1)
                    dve.wait_ge(free[w.bank("J", j)], w.turn("J", j) + 1)
                    return dve.tensor_tensor(m[:, t, :], m[:, t, :], hf[:, k % 2:k % 2 + 1, :], ALU.add)
                none = lambda i, k: None
                with_recurrence("ga", 4, none)
                with_recurrence("a", 6, set_merged)
                with_recurrence("gb", 8, none)

                def add_and_wait(i, k):
                    add_merged(i, k).then_inc(sems["dve_step"], w.given("dve_step"))
                    dve.wait_ge(sems["dve_step"], w.value("dve_step"))
                with_recurrence("b", None, add_and_wait)
                with_recurrence("gc", None, none)
                with w.loop("c", 2) as i:
                    for j in range(2):
                        for s in range(2):
                            lo(2 * j + s, 0), lo(2 * j + s, 1)
                        for n in range(2):
                            add_merged(i, 2 * j + n).then_inc(sems["m_f"], w.given("m_f"))
                        for n in range(2):
                            dve.wait_ge(sems["m_hi_done"], w.taken("m_hi_done"))
                            t = dyn(i, 4, 2 * j + n)
                            dve.tensor_tensor(h_lo[:, t, :], m[:, t, :], h_hi[:, t, :].bitcast(F32),
                                                     ALU.subtract).then_inc(sems["m_ready"], w.given("m_ready"))
                    w.go("S", 4), w.go("J", 4)
                with_recurrence("out", None, none)
                for j in range(1, 5):
                    dve.wait_ge(free[w.bank("J", -j)], w.turn("J", -j) + 1)
                total()
                for t in range(KT):
                    dve.wait_ge(sems["x_ready"], w.value("x_ready"))
                    dve.scalar_tensor_tensor(hf[:, t % 2, :], m[:, t, :], vec(l, "post", t), rs[:, :],
                                                  ALU.mult, ALU.mult).then_inc(sems["dve_step"], w.given("dve_step"))
                    dve.wait_ge(sems["dve_step"], w.value("dve_step"))
                    dve.tensor_tensor(x[:, t, :], x[:, t, :], hf[:, t % 2, :], ALU.add)\
                        .then_inc(sems["x_ready"], w.given("x_ready"))
            def col(r, n=1):
                return par[:, bass.ds(r, n)]

            def flat(t):
                return t.rearrange("p a n -> p (a n)")
            for t_ in (hp, ha, hb):
                dve.memset(t_[:, :, 0:8], 0.0)
            total()
            for t in range(KT):
                ins_ = dve.scalar_tensor_tensor(hp[:, t, 8:], x[:, t, :], col(ROW2["mix"] + t), rs[:, :],
                                                ALU.mult, ALU.mult)
            ins_.then_inc(sems["dve_step"], w.given("dve_step"))
            dve.wait_ge(sems["dve_step"], w.value("dve_step"))
            for g in range(4):
                two = slice(2 * g, 2 * g + 2)
                src, win = hp, 2 << g
                for n in range(g + 1):
                    d = 1 << n
                    dst = (ha, hb)[n % 2]
                    dve.tensor_tensor(dst[:, two, 8:], src[:, two, 8:], src[:, two, 8 - d:8 + TOK - d], ALU.add)\
                        .then_inc(sems["dve_step"], w.given("dve_step"))
                    dve.wait_ge(sems["dve_step"], w.value("dve_step"))
                    src = dst
                cnt = c["count"][:, 16 * g:16 * g + 16].unsqueeze(1).to_broadcast([P, 2, 16])
                dve.tensor_tensor(src[:, two, 8:24], src[:, two, 8:24], cnt, ALU.mult)\
                    .then_inc(sems["dve_step"], w.given("dve_step"))
                dve.wait_ge(sems["dve_step"], w.value("dve_step"))
                dve.tensor_tensor(hu[:, two, 0:16], src[:, two, 8:24], hp[:, two, 8:24], ALU.subtract)\
                    .then_inc(sems["dve_step"], w.given("dve_step"))
                dve.wait_ge(sems["dve_step"], w.value("dve_step"))
                dve.scalar_tensor_tensor(hu[:, two, 16:], src[:, two, 24:], 1.0 / win, hp[:, two, 24:],
                                                ALU.mult, ALU.subtract).then_inc(sems["u_f"], w.given("u_f", 2))
                dve.wait_ge(sems["u_f"], w.value("u_f"))
            for t in range(KT):
                dve.wait_ge(sems["u_hi_done"], w.taken("u_hi_done"))
                dve.tensor_tensor(h_lo[:, t, :], hu[:, t, :], h_hi[:, t, :].bitcast(F32), ALU.subtract)\
                    .then_inc(sems["u_ready"], w.given("u_ready"))
            for l in range(L):
                b = w.bank("K", l)
                dve.wait_ge(full[b], w.turn("K", l))
                dve.tensor_copy(flat(pf[:, 2 * l:2 * l + 2, :]), ps[b][:, :]).then_inc(free[w.bank("K", l)], 1)
                dve.wait_ge(free[w.bank("K", l)], w.turn("K", l) + 1)
                dve.drain().then_inc(sems["pf_ready"], w.given("pf_ready"))
            w.go("K", 2)
            for l in range(L):
                dve.wait_ge(sems["p_hi_done"], w.taken("p_hi_done"))
                dve.tensor_tensor(p_lo[:, 2 * l:2 * l + 2, :], pf[:, 2 * l:2 * l + 2, :],
                                         p_hi[:, 2 * l:2 * l + 2, :].bitcast(F32), ALU.subtract)\
                                             .then_inc(sems["p_ready2"], w.given("p_ready2"))
            for t in range(KT):
                b = w.bank("J", t)
                dve.wait_ge(full[b], w.turn("J", t))
                dve.scalar_tensor_tensor(x[:, t, :], acc(b), col(ROW2["scale"] + t), x[:, t, :],
                                                 ALU.mult, ALU.add).then_inc(free[w.bank("J", t)], 1)
            lo(0, 0), lo(0, 1)
            w.go("S", 1), w.go("J", 8)
            dve.drain().then_inc(sems["x_ready"], w.given("x_ready", KT))

            def add_x(label, slots):
                with w.loop(label, 2) as i:
                    for j in range(2):
                        for s in range(slots - 1):
                            lo(slots * j + s, 0), lo(slots * j + s, 1)
                        for n in range(2):
                            b = w.bank("J", 2 * j + n)
                            dve.wait_ge(full[b], w.turn("J", 2 * j + n))
                            t = dyn(i, 4, 2 * j + n)
                            dve.tensor_tensor(x[:, t, :], x[:, t, :], acc(b).rearrange("p (a n) -> p a n", a=1),
                                                      ALU.add).then_inc(free[w.bank("J", 2 * j + n)], 1)
                        lo(slots * (j + 1) - 1, 0), lo(slots * (j + 1) - 1, 1)
                    w.go("S", 2 * slots), w.go("J", 4)
                dve.drain().then_inc(sems["x_ready"], w.given("x_ready", KT))

            def ffn(l):
                norm_h(x, lambda t: col(ROW2["ffn"] + l * KT + t))
                with w.loop("up", FT // 2) as i:
                    for s, (u_, c0) in enumerate(((ua, 0), (ug, FT))):
                        for n in range(2):
                            lo(s, n)
                        for n in range(2):
                            dve.wait_ge(sems["act_part"], w.taken("act_part"))
                            b = w.bank("J", 2 * s + n)
                            for d in (1, 2):
                                ins_ = dve.scalar_tensor_tensor(u_[:, n, d:TOK], ps[b][:, 0:TOK - d],
                                                                col(i * 2 + (conv_row(l, 2 - d) + c0 + n)),
                                                                u_[:, n, d:TOK], ALU.mult, ALU.add)
                                if d == 1:
                                    ins_.then_inc(sems["dve_step"], w.given("dve_step"))
                                    dve.wait_ge(sems["dve_step"], w.value("dve_step"))
                            ins_.then_inc(free[w.bank("J", 2 * s + n)], 1)
                    for n in range(2):
                        dve.wait_ge(sems["sg_ready"], w.taken("sg_ready"))
                        dve.tensor_tensor(sg[:, n, :], sg[:, n, :], ug[:, n, :], ALU.mult)\
                            .then_inc(sems["dve_step"], w.given("dve_step"))
                        dve.wait_ge(sems["dve_step"], w.value("dve_step"))
                        dve.tensor_tensor(ua[:, n, :], ua[:, n, :], sg[:, n, :], ALU.mult)\
                            .then_inc(sems["f_f"], w.given("f_f"))
                    for n in range(2):
                        dve.wait_ge(sems["f_hi_done"], w.taken("f_hi_done"))
                        t = dyn(i, 2, n)
                        dve.tensor_tensor(y2_lo[:, t, :], ua[:, n:n + 1, :], y2_hi[:, t, :].bitcast(F32),
                                                 ALU.subtract).then_inc(sems["f_ready"], w.given("f_ready"))
                    w.go("S", 2), w.go("J", 4)
                add_x("down", 3)
                total()
                lo(0, 0), lo(0, 1)
                h_tiles(x, lambda t: col(ROW2["ple"] + l * KT + t))
                w.go("S", 1), w.go("J", 8)

                def ple(i, ahead):
                    for j in range(2):
                        if ahead:
                            lo(j, 0), lo(j, 1)
                        for n in range(2):
                            dve.wait_ge(free[w.bank("J", 2 * j + n)], w.turn("J", 2 * j + n) + 1)
                            t = dyn(i, 4, 2 * j + n)
                            dve.tensor_tensor(m[:, t, :], G[:, t, :], m[:, t, :], ALU.mult)\
                                .then_inc(sems["dve_step"], w.given("dve_step"))
                            dve.wait_ge(sems["dve_step"], w.value("dve_step"))
                            dve.tensor_tensor(x[:, t, :], x[:, t, :], m[:, t, :], ALU.add)
                    w.go("S", 2), w.go("J", 4)
                if l + 1 < L:
                    with w.loop("ple", 2) as i:
                        ple(i, True)
                else:
                    ple(0, True)
                    ple(1, False)
                dve.drain().then_inc(sems["x_ready"], w.given("x_ready", KT))
            ffn(0)
            norm_h(x, lambda t: col(ROW2["kv"] + t))
            dve.wait_ge(sems["nsa_in"], 96)
            dve.tensor_copy(ang[:, 0, :], posi[:, :]).then_inc(sems["dve_step"], w.given("dve_step"))
            dve.wait_ge(sems["dve_step"], w.value("dve_step"))
            dve.tensor_scalar(ang[:, 0, :], ang[:, 0, :], cst[:, CONST["freq"][0]:CONST["freq"][0] + 1], None, ALU.mult)\
                .then_inc(sems["dve_step"], w.given("dve_step"))
            dve.wait_ge(sems["dve_step"], w.value("dve_step"))
            BIG = 12582912.0
            dve.tensor_scalar(ang[:, 3, :], ang[:, 0, :], 1.0 / (2 * math.pi), BIG, ALU.mult, ALU.add)\
                .then_inc(sems["dve_step"], w.given("dve_step"))
            dve.wait_ge(sems["dve_step"], w.value("dve_step"))
            dve.tensor_scalar(ang[:, 3, :], ang[:, 3, :], -BIG, None, ALU.add)\
                .then_inc(sems["dve_step"], w.given("dve_step"))
            dve.wait_ge(sems["dve_step"], w.value("dve_step"))
            rest, parts = 2 * math.pi, []
            for bits in (5, 16):
                parts.append(math.floor(rest * 2.0 ** bits) / 2.0 ** bits)
                rest -= parts[-1]
            parts.append(rest)
            src = 0
            for part in parts:
                dve.scalar_tensor_tensor(ang[:, 1, :], ang[:, 3, :], -part, ang[:, src, :], ALU.mult, ALU.add)\
                    .then_inc(sems["dve_step"], w.given("dve_step"))
                dve.wait_ge(sems["dve_step"], w.value("dve_step"))
                src = 1
            dve.tensor_scalar(ang[:, 2, :], ang[:, 1, :], math.pi / 2, None, ALU.add)\
                .then_inc(sems["dve_step"], w.given("dve_step"))
            dve.wait_ge(sems["dve_step"], w.value("dve_step"))
            dve.tensor_scalar(ang[:, 3, :], ang[:, 2, :], math.pi, -2 * math.pi, ALU.is_gt, ALU.mult)\
                .then_inc(sems["dve_step"], w.given("dve_step"))
            dve.wait_ge(sems["dve_step"], w.value("dve_step"))
            dve.tensor_tensor(ang[:, 2, :], ang[:, 2, :], ang[:, 3, :], ALU.add)\
                .then_inc(sems["dve_step"], w.given("dve_step"))
            dve.wait_ge(sems["dve_step"], w.value("dve_step"))
            PI_ = 3.1415925
            dve.tensor_scalar(ang[:, 1:3, :], ang[:, 1:3, :], PI_, -PI_, ALU.min, ALU.max)\
                .then_inc(sems["pos_ready"], w.given("pos_ready"))
            lo(0, 0), lo(0, 1)
            dve.wait_ge(sems["sin_ready"], w.taken("sin_ready"))
            dve.tensor_scalar(sin2[:, :], sin2[:, :], cst[:, CONST["freq"][0] + 1:CONST["freq"][0] + 2], None, ALU.mult)\
                .then_inc(sems["dve_step"], w.given("dve_step"))
            dve.wait_ge(sems["dve_step"], w.value("dve_step"))
            for j in range(1, 6):
                lo(j, 0), lo(j, 1)
            w.go("S", 6), w.go("J", 12)

            def rotate2(t, key, n=TOK, cos_=None, sin_=None, tmp=None, more=False):
                b = w.bank("K")
                dve.wait_ge(full[b], w.turn("K"))
                tmp = hf[:, 0, :] if tmp is None else tmp
                cos_ = cos2[:, :] if cos_ is None else cos_
                sin_ = sin2[:, :] if sin_ is None else sin_
                src = acc(b, n)
                if more:
                    src = src.rearrange("p (g n) -> p g n", g=NG)
                dve.tensor_tensor(tmp, src, sin_, ALU.mult).then_inc(free[w.bank("K")], 1)
                dve.wait_ge(free[w.bank("K")], w.turn("K") + 1)
                dve.tensor_tensor(t, t, cos_, ALU.mult).then_inc(sems["dve_step"], w.given("dve_step"))
                dve.wait_ge(sems["dve_step"], w.value("dve_step"))
                dve.tensor_tensor(t, t, tmp, ALU.add).then_inc(sems["dve_step"], w.given("dve_step"))
                dve.wait_ge(sems["dve_step"], w.value("dve_step"))
                w.go("K", 1)
            dve.wait_ge(sems["nsa_zero"], 1)
            for t in range(4):
                rotate2(kr2[:, t, :], None)
            for a in range(2):
                for n in range(2):
                    for par_ in range(2):
                        ins_ = dve.tensor_copy(kz[64 * par_:64 * par_ + 64, par_, n:4:2, a, :],
                                               kr2[64 * n:64 * n + 64, 2 * a:2 * a + 2, :])
            ins_.then_inc(sems["k2_ready"], w.given("k2_ready"))
            b = w.bank("K")
            dve.wait_ge(full[b], w.turn("K"))
            dve.tensor_copy(stat[:, 0, 0, 0:2], ps[b][:, 128:130]).then_inc(sems["dve_step"], w.given("dve_step"))
            dve.wait_ge(sems["dve_step"], w.value("dve_step"))
            for n in range(2):
                ins_ = dve.tensor_scalar(ge[:, n, :], ps[b][:, 64 * n:64 * n + 60], stat[:, 0, 0, n:n + 1], None, ALU.add)
            ins_.then_inc(free[w.bank("K")], 1)
            dve.wait_ge(free[w.bank("K")], w.turn("K") + 1)
            w.go("K", 1)
            dve.tensor_tensor(ge[:, 2:4, :], ge[:, 0:2, :], ge[:, 0:2, :], ALU.mult)\
                .then_inc(sems["dve_step"], w.given("dve_step"))
            dve.wait_ge(sems["dve_step"], w.value("dve_step"))
            dve.tensor_scalar(ge[:, 2:4, :], ge[:, 2:4, :], 0.044715, 1.0, ALU.mult, ALU.add)\
                .then_inc(sems["dve_step"], w.given("dve_step"))
            dve.wait_ge(sems["dve_step"], w.value("dve_step"))
            dve.tensor_tensor(ge[:, 2:4, :], ge[:, 2:4, :], ge[:, 0:2, :], ALU.mult)\
                .then_inc(sems["gelu_ask"], w.given("gelu_ask"))
            h_tiles(x, lambda t: col(ROW2["mix"] + KT + t))
            dve.wait_ge(sems["gelu_done"], w.taken("gelu_done"))
            dve.tensor_scalar(ge[:, 2:4, :], ge[:, 2:4, :], 1.0, 0.5, ALU.add, ALU.mult)\
                .then_inc(sems["dve_step"], w.given("dve_step"))
            dve.wait_ge(sems["dve_step"], w.value("dve_step"))
            dve.tensor_tensor(ge[:, 2:4, :], ge[:, 2:4, :], ge[:, 0:2, :], ALU.mult)\
                .then_inc(sems["ge_ready"], w.given("ge_ready"))
            lo(0, 0), lo(0, 1)
            w.go("S", 1), w.go("J", 2)
            dve.memset(kcz[:, :, :], 0.0)
            w.go("K", 2)
            ends = slice(31, TOK, 16)
            e_cos, e_sin = (t_[:, ends].unsqueeze(1).to_broadcast([P, NG, NCMP]) for t_ in (cos2, sin2))
            w.n["kc_ready"] += 1
            kc3 = kcd[:, :].rearrange("p (g n) -> p g n", g=NG)
            rotate2(kc3, None, 60, e_cos, e_sin, hf[:, 0, 0:60].rearrange("p (g n) -> p g n", g=NG), more=True)
            dve.tensor_copy(kcz[0:64, 0, :], kcd[0:64, :])
            dve.tensor_copy(kcz[64:P, 1, :], kcd[64:P, :]).then_inc(sems["vc_ready"], w.given("vc_ready"))
            with w.loop("q2", 2) as i:
                for j in range(2):
                    lo(j, 0), lo(j, 1)
                w.go("S", 2), w.go("J", 4)
            for t in range(KT):
                rotate2(q2[:, t, :], None)
                dve.drain().then_inc(sems["q2_ready"], w.given("q2_ready"))

            def softmax2(g):
                r = g % 2
                b = w.bank("K", 0)
                dve.wait_ge(full[b], w.turn("K", 0))
                dve.tensor_scalar(Tc[:, r, :, :, :].rearrange("p t n k -> p (t n) k")[:, :, 0:NCMP],
                                       ps[b][:, 0:128].rearrange("p (a k) -> p a k", a=8)[:, :, 0:NCMP],
                                       SCALE2, None, ALU.mult).then_inc(sems["dve_step"], w.given("dve_step"))
                dve.wait_ge(sems["dve_step"], w.value("dve_step"))
                dve.memset(Tc[:, r, :, :, NCMP:16], 0.0).then_inc(free[w.bank("K", 0)], 1)
                dve.wait_ge(free[w.bank("K", 0)], w.turn("K", 0) + 1)
                for u in range(2):
                    b = w.bank("K", 1 + u)
                    dve.wait_ge(full[b], w.turn("K", 1 + u))
                    dve.scalar_tensor_tensor(
                        T0[:, r, 2 * u:2 * u + 2, :, :].rearrange("p n a k -> p (n a) k"),
                        ps[b][:, :].rearrange("p (a k) -> p a k", a=4), SCALE2,
                        c["causal1"][:, P:TOK].unsqueeze(1).to_broadcast([P, 4, P]), ALU.mult, ALU.add)\
                            .then_inc(free[w.bank("K", 1 + u)], 1)
                for n in range(4):
                    b = w.bank("K", 3 + n)
                    dve.wait_ge(full[b], w.turn("K", 3 + n))
                    dve.scalar_tensor_tensor(
                        T1[:, r, n, :, :], ps[b][:, :].rearrange("p (a k) -> p a k", a=2), SCALE2,
                        c["causal1"].unsqueeze(1).to_broadcast([P, 2, TOK]), ALU.mult, ALU.add)\
                            .then_inc(free[w.bank("K", 3 + n)], 1)
                for j in range(3, 7):
                    dve.wait_ge(free[w.bank("K", j)], w.turn("K", j) + 1)
                w.go("K", 7)
                tc = Tc[:, r, :, :, :]
                for qt in range(TT):
                    mk = c["cmp1" if qt else "cmp0"].unsqueeze(1).to_broadcast([P, 4, 16])
                    off = c["cmo1" if qt else "cmo0"].unsqueeze(1).to_broadcast([P, 4, 16])
                    dve.tensor_tensor(tc[:, qt], tc[:, qt], mk, ALU.mult)\
                        .then_inc(sems["dve_step"], w.given("dve_step"))
                    dve.wait_ge(sems["dve_step"], w.value("dve_step"))
                    dve.tensor_tensor(tc[:, qt], tc[:, qt], off, ALU.add)\
                        .then_inc(sems["dve_step"], w.given("dve_step"))
                    dve.wait_ge(sems["dve_step"], w.value("dve_step"))
                tc8 = tc.rearrange("p t n k -> p (t n) k")
                dve.tensor_reduce(stat[:, r, 0, 16:24], tc8, AX.X, ALU.max)\
                    .then_inc(sems["dve_step"], w.given("dve_step"))
                dve.wait_ge(sems["dve_step"], w.value("dve_step"))
                dve.tensor_tensor(tc8, tc8, stat[:, r, 0, 16:24].unsqueeze(2).to_broadcast([P, 8, 16]), ALU.subtract)\
                    .then_inc(sems["dve_step"], w.given("dve_step"))
                dve.wait_ge(sems["dve_step"], w.value("dve_step"))
                dve.tensor_reduce(stat[:, r, 0, 0:8], T0[:, r].rearrange("p n a k -> p (n a) k"), AX.X, ALU.max)\
                    .then_inc(sems["dve_step"], w.given("dve_step"))
                dve.wait_ge(sems["dve_step"], w.value("dve_step"))
                dve.tensor_reduce(stat[:, r, 0, 8:16], T1[:, r].rearrange("p n a k -> p (n a) k"), AX.X, ALU.max)\
                    .then_inc(sems["dve_step"], w.given("dve_step"))
                dve.wait_ge(sems["dve_step"], w.value("dve_step"))
                dve.tensor_scalar(stat[:, r, 1, 0:16], stat[:, r, 0, 0:16], -1.0, None, ALU.mult)\
                    .then_inc(sems["t_ready"], w.given("t_ready"))

            def weigh2(g):
                r = g % 2
                dve.wait_ge(sems["t_exp"], w.taken("t_exp"))
                tc = Tc[:, r, :, :, :]
                for qt in range(TT):
                    mk = c["cmp1" if qt else "cmp0"].unsqueeze(1).to_broadcast([P, 4, 16])
                    dve.tensor_tensor(tc[:, qt], tc[:, qt], mk, ALU.mult)\
                        .then_inc(sems["dve_step"], w.given("dve_step"))
                    dve.wait_ge(sems["dve_step"], w.value("dve_step"))
                tc8 = tc.rearrange("p t n k -> p (t n) k")
                dve.tensor_reduce(stat[:, r, 2, 16:24], tc8, AX.X, ALU.add)\
                    .then_inc(sems["dve_step"], w.given("dve_step"))
                dve.wait_ge(sems["dve_step"], w.value("dve_step"))
                dve.tensor_scalar(stat[:, r, 2, 16:24], stat[:, r, 2, 16:24], 1e-30, None, ALU.max)\
                    .then_inc(sems["dve_step"], w.given("dve_step"))
                dve.wait_ge(sems["dve_step"], w.value("dve_step"))
                dve.reciprocal(stat[:, r, 3, :], stat[:, r, 2, :]).then_inc(sems["dve_step"], w.given("dve_step"))
                dve.wait_ge(sems["dve_step"], w.value("dve_step"))
                dve.tensor_tensor(stat[:, r, 3, 0:16].rearrange("p (t n a) -> p t n a", t=2, n=4),
                                       stat[:, r, 3, 0:16].rearrange("p (t n a) -> p t n a", t=2, n=4),
                                       gt[:, :, 12 * g:12 * g + 12].rearrange("p t (n a) -> p t n a", a=3)[:, :, :, 1:3],
                                       ALU.mult).then_inc(sems["dve_step"], w.given("dve_step"))
                dve.wait_ge(sems["dve_step"], w.value("dve_step"))
                dve.tensor_tensor(stat[:, r, 3, 16:24].rearrange("p (t n) -> p t n", t=2),
                                       stat[:, r, 3, 16:24].rearrange("p (t n) -> p t n", t=2),
                                       gt[:, :, 12 * g:12 * g + 12].rearrange("p t (n a) -> p t n a", a=3)[:, :, :, 0],
                                       ALU.mult).then_inc(sems["dve_step"], w.given("dve_step"))
                dve.wait_ge(sems["dve_step"], w.value("dve_step"))
                dve.tensor_tensor(tc8, tc8, stat[:, r, 3, 16:24].unsqueeze(2).to_broadcast([P, 8, 16]), ALU.mult)
                for qt, (T, n) in enumerate(((T0, P), (T1, TOK))):
                    t8 = T[:, r].rearrange("p n a k -> p (n a) k")
                    ins_ = dve.tensor_tensor(t8, t8, stat[:, r, 3, 8 * qt:8 * qt + 8].unsqueeze(2).to_broadcast([P, 8, n]),
                                             ALU.mult)
                ins_.then_inc(sems["t_done"], w.given("t_done"))
                dve.wait_ge(sems["t_done"], w.value("t_done"))
            softmax2(0)
            for g in range(NG):
                if g + 1 < NG:
                    softmax2(g + 1)
                weigh2(g)
                w.go("K", 10)
            for u in range(KT // 2):
                b = w.bank("K", u)
                dve.wait_ge(full[b], w.turn("K", u))
                dve.wait_ge(sems["o_hi_done"], w.taken("o_hi_done"))
                dve.tensor_tensor(flat(h_lo[:, 2 * u:2 * u + 2, :]), ps[b][:, :],
                                          flat(h_hi[:, 2 * u:2 * u + 2, :]).bitcast(F32), ALU.subtract)\
                                              .then_inc(free[w.bank("K", u)], 1)
            w.go("K", 4)
            dve.drain().then_inc(sems["o_split"], w.given("o_split", KT))
            add_x("o2", 1)
            ffn(1)
            total()
            for t in range(KT):
                ins_ = dve.scalar_tensor_tensor(m[:, t, :], x[:, t, :], col(ROW2["final"] + t), rs[:, :],
                                                ALU.mult, ALU.mult)
            ins_.then_inc(sems["final_ready"], w.given("final_ready"))
            for k in range(4):
                b = w.bank("K", k)
                dve.wait_ge(full[b], w.turn("K", k))
                dve.tensor_copy(flat(x[:, 2 * k:2 * k + 2, :]), ps[b][:, :]).then_inc(free[w.bank("K", k)], 1)
            dve.drain().then_inc(sems["out_ready"], 1)

STEPS = {'act.a': {'J': 4, 'S': 2, 'sqrt_ask': 1, 'sqrt_done': 1, 'yc_f': 1, 'yc_hi_done': 1},
 'act.b': {'J': 4, 'S': 2},
 'act.c': {'J': 4, 'S': 4, 'm_f': 4, 'm_hi_done': 4, 'w_used': 2},
 'act.down': {'J': 4, 'S': 6, 'sq': 4, 'w_used': 4},
 'act.ga': {'J': 4, 'S': 2, 'sqrt_ask': 1, 'sqrt_done': 1, 'table_in': 1, 'yc_f': 1, 'yc_hi_done': 1},
 'act.gb': {'J': 4, 'S': 2, 'sqrt_ask': 1, 'sqrt_done': 1, 'table_in': 1, 'yc_f': 1, 'yc_hi_done': 1},
 'act.gc': {'J': 4, 'S': 2, 'table_in': 1},
 'act.layer': {'J': 140,
               'K': 56,
               'S': 68,
               'act_part': 36,
               'c_hi_done': 5,
               'cq_f': 5,
               'cq_raw': 5,
               'h_hi_done': 8,
               'hf_ready': 8,
               'ln_part': 2,
               'ln_rstd': 1,
               'ln_sq': 1,
               'm_f': 8,
               'm_hi_done': 8,
               'mean_sq': 2,
               'ms_c': 1,
               'p_exp': 2,
               'rstd': 2,
               'rstd_c': 1,
               's_ready': 2,
               'sq': 10,
               'sqrt_ask': 10,
               'sqrt_done': 10,
               'table_in': 13,
               'tanh_ready': 10,
               'w_used': 4,
               'x_ready': 8,
               'y_f': 8,
               'y_hi_done': 16,
               'yc_f': 10,
               'yc_hi_done': 10},
 'act.o2': {'J': 4, 'S': 2, 'sq': 4},
 'act.out': {'J': 4, 'S': 2, 'sq': 4},
 'act.ple': {'J': 4, 'S': 2, 'table_in': 1},
 'act.q2': {'J': 4, 'S': 2},
 'act.up': {'J': 4, 'S': 2, 'act_part': 4, 'f_f': 2, 'f_hi_done': 2, 'f_ready': 2, 'sg_ready': 2, 'table_in': 1},
 'act.uz': {'J': 4, 'S': 2, 'act_part': 2, 'sqrt_ask': 1, 'sqrt_done': 1, 'yc_f': 1, 'yc_hi_done': 1},
 'act.v': {'J': 4, 'S': 2},
 'act.xz': {'J': 4, 'S': 2, 'act_part': 4, 'table_in': 1},
 'act.zb': {'J': 4, 'S': 2, 'act_part': 4, 'table_in': 1},
 'dve.a': {'J': 4,
           'S': 2,
           'dve_step': 4,
           'sqrt_ask': 1,
           'sqrt_done': 1,
           'sqrt_own': 1,
           'tanh_ready': 1,
           'yc_f': 1,
           'yc_hi_done': 1,
           'yc_ready': 1},
 'dve.b': {'J': 4, 'S': 2, 'dve_step': 4},
 'dve.c': {'J': 4, 'S': 4, 'm_f': 4, 'm_hi_done': 4, 'm_ready': 4},
 'dve.down': {'J': 4, 'S': 6},
 'dve.ga': {'J': 4,
            'S': 2,
            'dve_step': 4,
            'sqrt_ask': 1,
            'sqrt_done': 1,
            'sqrt_own': 1,
            'tanh_ready': 1,
            'yc_f': 1,
            'yc_hi_done': 1,
            'yc_ready': 1},
 'dve.gb': {'J': 4,
            'S': 2,
            'dve_step': 4,
            'sqrt_ask': 1,
            'sqrt_done': 1,
            'sqrt_own': 1,
            'tanh_ready': 1,
            'yc_f': 1,
            'yc_hi_done': 1,
            'yc_ready': 1},
 'dve.gc': {'J': 4, 'S': 2},
 'dve.layer': {'J': 140,
               'K': 56,
               'S': 68,
               'act_part': 36,
               'c_hi_done': 5,
               'c_ready': 5,
               'cq_f': 5,
               'dve_step': 90,
               'h_hi_done': 8,
               'h_ready': 8,
               'hf_ready': 8,
               'ln_in': 32,
               'ln_part': 2,
               'ln_rstd': 1,
               'ln_sq': 1,
               'm_f': 8,
               'm_hi_done': 8,
               'm_ready': 8,
               'mean_sq': 2,
               'ms_c': 1,
               'p_exp': 2,
               'p_ready': 2,
               'q_ready': 6,
               'rstd': 2,
               'rstd_c': 1,
               's_ready': 2,
               'sqrt_ask': 10,
               'sqrt_done': 10,
               'sqrt_own': 10,
               'tanh_ready': 10,
               'vn_ready': 1,
               'wsT_ready': 1,
               'ws_in': 32,
               'x_ready': 8,
               'y_f': 8,
               'y_hi_done': 16,
               'y_ready': 16,
               'yc_f': 10,
               'yc_hi_done': 10,
               'yc_ready': 10},
 'dve.o2': {'J': 4, 'S': 2},
 'dve.out': {'J': 4, 'S': 2},
 'dve.ple': {'J': 4, 'S': 2, 'dve_step': 4},
 'dve.q2': {'J': 4, 'S': 2},
 'dve.up': {'J': 4, 'S': 2, 'act_part': 4, 'dve_step': 6, 'f_f': 2, 'f_hi_done': 2, 'f_ready': 2, 'sg_ready': 2},
 'dve.uz': {'J': 4,
            'S': 2,
            'act_part': 2,
            'dve_step': 4,
            'sqrt_ask': 1,
            'sqrt_done': 1,
            'sqrt_own': 1,
            'tanh_ready': 1,
            'yc_f': 1,
            'yc_hi_done': 1,
            'yc_ready': 1},
 'dve.v': {'J': 4, 'S': 2},
 'dve.xz': {'J': 4, 'S': 2, 'act_part': 4, 'dve_step': 4},
 'dve.zb': {'J': 4, 'S': 2, 'act_part': 4},
 'pe.a': {'J': 4, 'S': 2},
 'pe.b': {'J': 4, 'S': 2},
 'pe.c': {'J': 4, 'S': 4, 'w_used': 2},
 'pe.down': {'J': 4, 'S': 6, 'w_used': 4},
 'pe.ga': {'J': 4, 'S': 2},
 'pe.gb': {'J': 4, 'S': 2},
 'pe.gc': {'J': 4, 'S': 2},
 'pe.layer': {'J': 140,
              'K': 56,
              'S': 68,
              'attn_dead': 1,
              'b_used': 1,
              'c_ready': 5,
              'conv_ready': 10,
              'cq_raw': 5,
              'gate_in': 640,
              'h_ready': 8,
              'm_ready': 8,
              'p_ready': 2,
              'q_ready': 6,
              'sq': 10,
              'vn_ready': 1,
              'w_used': 4,
              'wsT_ready': 1,
              'ws_in': 32,
              'y_ready': 16,
              'yc_ready': 10},
 'pe.o2': {'J': 4, 'S': 2},
 'pe.out': {'J': 4, 'S': 2},
 'pe.ple': {'J': 4, 'S': 2},
 'pe.q2': {'J': 4, 'S': 2},
 'pe.up': {'J': 4, 'S': 2},
 'pe.uz': {'J': 4, 'S': 2},
 'pe.v': {'J': 4, 'S': 2},
 'pe.xz': {'J': 4, 'S': 2},
 'pe.zb': {'J': 4, 'S': 2},
 'pool.layer': {'attn_dead': 1, 'b_used': 1, 'gate_zero': 1},
 'sp.a': {'S': 2},
 'sp.b': {'S': 2},
 'sp.c': {'S': 2},
 'sp.down': {'S': 6},
 'sp.ga': {'S': 2},
 'sp.gb': {'S': 2},
 'sp.gc': {'S': 2},
 'sp.layer': {'S': 68},
 'sp.o2': {'S': 2},
 'sp.out': {'S': 2},
 'sp.ple': {'S': 2},
 'sp.q2': {'S': 2},
 'sp.up': {'S': 2},
 'sp.uz': {'S': 2},
 'sp.v': {'S': 2},
 'sp.xz': {'S': 2},
 'sp.zb': {'S': 2}}

INPUTS = ['x', 'pre_norm_g', 'w_in', 'gm_ln_g', 'gm_ln_b', 'gm_ws', 'gm_bs', 'mla_q_norm_g', 'mla_w_uq', 'mla_kv_norm_g', 'mla_w_ukv', 'lru_conv_w', 'lru_conv_b', 'lru_w_a', 'lru_b_a', 'lru_w_x', 'lru_b_x', 'lru_lambda', 'w_proj_a', 'w_proj_b', 'w_proj_c', 'w_out', 'post_norm_g', 'p_2', 'positions_2', 'norm_mix_2', 'pool_w_2', 'pool_scale_2', 'norm_kv_2', 'w_kv_2', 'cmp_pos_k_2', 'cmp_w1_k_2', 'cmp_w2_k_2', 'cmp_pos_v_2', 'cmp_w1_v_2', 'cmp_w2_v_2', 'w_in_b_2', 'w_out_b_2', 'norm_ffn_2', 'ffn_up_2', 'ffn_conv_2', 'ffn_conv_b_2', 'ffn_down_2', 'norm_ple_2', 'ple_gate_2', 'ple_proj_2', 'norm_final_2']


def kernel(**inputs):
    import numpy as _np
    import concourse.bacc as _bacc
    from concourse import mybir as _mybir
    from concourse.bass_utils import run_bass_kernel_spmd as _run

    nc = _bacc.Bacc("TRN2", target_bir_lowering=False, num_devices=1)
    arrays, ins = {}, {}
    for name in INPUTS:
        a = _np.ascontiguousarray(inputs[name])
        arrays[f"in_{name}"] = a
        ins[name] = nc.dram_tensor(f"in_{name}", a.shape, _mybir.dt.from_np(a.dtype), kind="ExternalInput").ap()
    a = shape_constants()
    arrays["in_shape_constants"] = a
    ins["shape_constants"] = nc.dram_tensor("in_shape_constants", a.shape, _mybir.dt.float32, kind="ExternalInput").ap()
    out = nc.dram_tensor("out_dram", (1, TOK, D), _mybir.dt.float32, kind="ExternalOutput").ap()
    program(nc, STEPS, ins, out)
    r = _run(nc, [arrays], core_ids=[0])
    return r.results[0]["out_dram"]
```
